# Optimizing a Trainium2 kernel written in Bass

```python
import jax
import jax.numpy as jnp
from jax import lax
import numpy as np

D_MODEL = 1024
BATCH = 1
SEQ = 512
DEPTH = 1
DEC_BATCH = 8
DEC_SEQ = 1
PAST_LEN = 4096
PAGE_SIZE = 128

MIX_W = D_MODEL
GROUP_W = MIX_W // 4
CONF_K = 31
CONF_COLS = 2 * GROUP_W
RWKV_HEAD = 64
RWKV_H = GROUP_W // RWKV_HEAD
DECAY_LORA = 32
AAA_LORA = 32
GATE_LORA = 64
RWKV_SIZES = (GROUP_W, DECAY_LORA, GROUP_W, GROUP_W, AAA_LORA, GATE_LORA)
RWKV_COLS = GROUP_W * 3 + DECAY_LORA + AAA_LORA + GATE_LORA
RWKV_GN_EPS = 64e-5
SC_K = 3
SC_COLS = 3 * GROUP_W
POOL_WINDOWS = (2, 4, 8, 16)
POOL_G = 4
POOL_CH = GROUP_W // POOL_G
POOL_BUF = 15
POOL_COLS = GROUP_W
IN_SIZES = (CONF_COLS, RWKV_COLS, SC_COLS, POOL_COLS)
IN_COLS = CONF_COLS + RWKV_COLS + SC_COLS + POOL_COLS
N_KEYS = 128
N_EXPERTS = N_KEYS * N_KEYS
PEER_HEADS = 8
PEER_TOPK = 16
PEER_QDIM = 256
PEER_BLOCK = 128
RMS_EPS = 1e-6
LN_EPS = 1e-5

kernel_name = 'hybrid_conformer_rwkv7_shortconv_pool_peer_step'

def _offsets(sizes):
    out, acc = [], 0
    for s in sizes[:-1]:
        acc += s
        out.append(acc)
    return out

def rmsnorm(x, g):
    xf = x.astype(jnp.float32)
    y = xf * lax.rsqrt(jnp.mean(xf * xf, axis=-1, keepdims=True) + RMS_EPS) * g.astype(jnp.float32)
    return y.astype(x.dtype)

def layernorm(x, g, b, eps):
    mu = jnp.mean(x, axis=-1, keepdims=True)
    xc = x - mu
    var = jnp.mean(xc * xc, axis=-1, keepdims=True)
    return xc * lax.rsqrt(var + eps) * g + b

def causal_dwconv(u, buf, w):
    ext = jnp.concatenate([buf, u], axis=1)
    k = w.shape[0]
    y = lax.conv_general_dilated(ext, w[:, None, :], window_strides=(1,), padding='VALID',
                                 dimension_numbers=('NWC', 'WIO', 'NWC'),
                                 feature_group_count=u.shape[-1])
    return y, ext[:, ext.shape[1] - (k - 1):]

def multiscale_pool(u, buf, start_pos, pool_w, pool_scale):
    bsz, t, c = u.shape
    ext = jnp.concatenate([buf, u], axis=1)
    cs = jnp.concatenate([jnp.zeros((bsz, 1, c), jnp.float32), jnp.cumsum(ext, axis=1)], axis=1)
    pos = start_pos + jnp.arange(t)
    outs = []
    for gi, win in enumerate(POOL_WINDOWS):
        lo, hi = gi * POOL_CH, (gi + 1) * POOL_CH
        wsum = cs[:, POOL_BUF + 1:POOL_BUF + 1 + t, lo:hi] - cs[:, POOL_BUF + 1 - win:POOL_BUF + 1 - win + t, lo:hi]
        cnt = jnp.minimum(win, pos + 1).astype(jnp.float32)[None, :, None]
        pooled = wsum / cnt - u[:, :, lo:hi]
        outs.append(jnp.einsum('btc,cd->btd', pooled, pool_w[gi]))
    y = jnp.concatenate(outs, axis=-1) * pool_scale
    return y, ext[:, ext.shape[1] - POOL_BUF:]

def wkv7_scan(r, w, k, v, kk, a, s0):
    def step(s, inp):
        r_t, w_t, k_t, v_t, kk_t, a_t = inp
        sa = jnp.einsum('bhij,bhj->bhi', s, -kk_t)
        s = (s * w_t[:, :, None, :] + sa[..., None] * (kk_t * a_t)[:, :, None, :]
             + v_t[..., None] * k_t[:, :, None, :])
        y = jnp.einsum('bhij,bhj->bhi', s, r_t)
        return s, y
    xs = tuple(jnp.moveaxis(z, 1, 0) for z in (r, w, k, v, kk, a))
    s_fin, ys = lax.scan(step, s0, xs)
    return jnp.moveaxis(ys, 0, 1), s_fin

def rwkv7_time_mix(p, shift_buf, s0, wl):
    bsz, t, _ = p.shape
    prev = jnp.concatenate([shift_buf[:, None, :], p[:, :-1]], axis=1)
    xs = p + (prev - p) * wl['rwkv_mu']
    r, w_lo, k, v, a_lo, g_lo = jnp.split(xs, _offsets(RWKV_SIZES), axis=-1)
    w = -jax.nn.softplus(-(wl['rwkv_w0'] + jnp.matmul(jnp.tanh(w_lo), wl['rwkv_w2']))) - 0.5
    decay = jnp.exp(-jnp.exp(w))
    a = jax.nn.sigmoid(wl['rwkv_a0'] + jnp.matmul(a_lo, wl['rwkv_a2']))
    g = jnp.matmul(jax.nn.sigmoid(g_lo), wl['rwkv_g2'])

    def heads(z):
        return z.reshape(bsz, t, RWKV_H, RWKV_HEAD)

    kk = heads(k * wl['rwkv_k_k'])
    kk = kk * lax.rsqrt(jnp.maximum(jnp.sum(kk * kk, axis=-1, keepdims=True), 1e-24))
    k = k * (1.0 + (a - 1.0) * wl['rwkv_k_a'])
    rh, kh, vh, ah, dh = heads(r), heads(k), heads(v), heads(a), heads(decay)
    yh, s_fin = wkv7_scan(rh, dh, kh, vh, kk, ah, s0)
    yh = layernorm(yh, wl['rwkv_ln_g'].reshape(RWKV_H, RWKV_HEAD),
                   wl['rwkv_ln_b'].reshape(RWKV_H, RWKV_HEAD), RWKV_GN_EPS)
    yh = yh + jnp.sum(rh * kh * wl['rwkv_r_k'], axis=-1, keepdims=True) * vh
    y = yh.reshape(bsz, t, GROUP_W) * g
    return y, p[:, -1], s_fin

def token_mixers(h, bufs, start_pos, wl):
    f32 = jnp.float32
    conf_buf, shift_buf, wkv_s, sc_buf, pool_buf = bufs
    z = jnp.matmul(h, wl['w_in']).astype(f32)
    za, zb, zc, zd = jnp.split(z, _offsets(IN_SIZES), axis=-1)
    glu = za[..., :GROUP_W] * jax.nn.sigmoid(za[..., GROUP_W:])
    ca, new_conf = causal_dwconv(glu, conf_buf.astype(f32), wl['conf_dw_w'].astype(f32))
    ya = jax.nn.silu(layernorm(ca + wl['conf_dw_b'], wl['conf_ln_g'], wl['conf_ln_b'], LN_EPS))
    yb, new_shift, new_wkv = rwkv7_time_mix(zb, shift_buf.astype(f32), wkv_s.astype(f32), wl)
    gate_b, gate_c, hc = jnp.split(zc, 3, axis=-1)
    cc, new_sc = causal_dwconv(gate_c * hc, sc_buf.astype(f32), wl['sc_conv_w'].astype(f32))
    yc = gate_b * cc
    yd, new_pool = multiscale_pool(zd, pool_buf.astype(f32), start_pos,
                                   wl['pool_w'].astype(f32), wl['pool_scale'])
    y = jnp.concatenate([ya, yb, yc, yd], axis=-1).astype(h.dtype)
    out = jnp.matmul(y, wl['w_out'])
    dt = h.dtype
    return out, (new_conf.astype(dt), new_shift.astype(dt), new_wkv.astype(dt),
                 new_sc.astype(dt), new_pool.astype(dt))

def peer_ffn(x, wq, k1, k2, u_tab, v_tab):
    f32 = jnp.float32
    bsz, t, d = x.shape
    xt = x.reshape(-1, d)
    n = xt.shape[0]
    q = jnp.matmul(xt, wq).astype(f32).reshape(n, PEER_HEADS, 2, PEER_QDIM // 2)
    s1 = jnp.einsum('nhc,hkc->nhk', q[:, :, 0], k1.astype(f32))
    s2 = jnp.einsum('nhc,hkc->nhk', q[:, :, 1], k2.astype(f32))
    v1, i1 = lax.top_k(s1, PEER_TOPK)
    v2, i2 = lax.top_k(s2, PEER_TOPK)
    cand = (v1[..., :, None] + v2[..., None, :]).reshape(n, PEER_HEADS, PEER_TOPK * PEER_TOPK)
    sc, pos = lax.top_k(cand, PEER_TOPK)
    e = (jnp.take_along_axis(i1, pos // PEER_TOPK, axis=-1) * N_KEYS
         + jnp.take_along_axis(i2, pos % PEER_TOPK, axis=-1))
    g = jax.nn.softmax(sc, axis=-1)
    e = e.reshape(n, PEER_HEADS * PEER_TOPK)
    g = g.reshape(n, PEER_HEADS * PEER_TOPK)
    pad = (-n) % PEER_BLOCK
    xp = jnp.pad(xt, ((0, pad), (0, 0)))
    ep = jnp.pad(e, ((0, pad), (0, 0)))
    gp = jnp.pad(g, ((0, pad), (0, 0)))
    nb = (n + pad) // PEER_BLOCK

    def block(args):
        xb, eb, gb = args
        hsel = jnp.einsum('tsd,td->ts', u_tab[eb], xb).astype(f32)
        wgt = gb * jax.nn.gelu(hsel, approximate=False)
        return jnp.einsum('ts,tsd->td', wgt.astype(v_tab.dtype), v_tab[eb])

    out = lax.map(block, (xp.reshape(nb, PEER_BLOCK, d), ep.reshape(nb, PEER_BLOCK, -1),
                          gp.reshape(nb, PEER_BLOCK, -1)))
    return out.reshape(-1, d)[:n].reshape(bsz, t, d).astype(x.dtype)

def setup_inputs(seed: int = 0) -> dict:
    key = jax.random.key(seed)
    ks = list(jax.random.split(key, 40))
    f32 = jnp.float32

    def nrm(i, shape, scale):
        return jax.random.normal(ks[i], shape, f32) * scale

    L = DEPTH
    return {
        'x_prompt': nrm(0, (BATCH, SEQ, D_MODEL), 1.0),
        'x_sample': nrm(1, (DEC_BATCH, DEC_SEQ, D_MODEL), 1.0),
        'state_conformer': nrm(2, (L, DEC_BATCH, CONF_K - 1, GROUP_W), 0.5),
        'state_rwkv_shift': nrm(3, (L, DEC_BATCH, RWKV_COLS), 1.0),
        'state_rwkv_wkv': nrm(4, (L, DEC_BATCH, RWKV_H, RWKV_HEAD, RWKV_HEAD), 0.3),
        'state_shortconv': nrm(5, (L, DEC_BATCH, SC_K - 1, GROUP_W), 0.7),
        'state_pool': nrm(6, (L, DEC_BATCH, POOL_BUF, GROUP_W), 1.0),
        'norm1_g': 1.0 + nrm(7, (L, D_MODEL), 0.05),
        'norm2_g': 1.0 + nrm(8, (L, D_MODEL), 0.05),
        'final_norm_g': 1.0 + nrm(9, (D_MODEL,), 0.05),
        'w_in': nrm(10, (L, D_MODEL, IN_COLS), D_MODEL ** -0.5),
        'conf_dw_w': nrm(11, (L, CONF_K, GROUP_W), CONF_K ** -0.5),
        'conf_dw_b': nrm(12, (L, GROUP_W), 0.02),
        'conf_ln_g': 1.0 + nrm(13, (L, GROUP_W), 0.05),
        'conf_ln_b': nrm(14, (L, GROUP_W), 0.02),
        'rwkv_mu': jax.random.uniform(ks[15], (L, RWKV_COLS), f32),
        'rwkv_w0': jax.random.uniform(ks[16], (L, GROUP_W), f32, -4.0, 1.0),
        'rwkv_w2': nrm(17, (L, DECAY_LORA, GROUP_W), 0.1),
        'rwkv_a0': nrm(18, (L, GROUP_W), 0.1),
        'rwkv_a2': nrm(19, (L, AAA_LORA, GROUP_W), 0.5 * AAA_LORA ** -0.5),
        'rwkv_g2': nrm(20, (L, GATE_LORA, GROUP_W), GATE_LORA ** -0.5),
        'rwkv_k_k': 0.85 + nrm(21, (L, GROUP_W), 0.05),
        'rwkv_k_a': 1.0 + nrm(22, (L, GROUP_W), 0.05),
        'rwkv_r_k': nrm(23, (L, RWKV_H, RWKV_HEAD), 0.1),
        'rwkv_ln_g': 1.0 + nrm(24, (L, GROUP_W), 0.05),
        'rwkv_ln_b': nrm(25, (L, GROUP_W), 0.02),
        'sc_conv_w': nrm(26, (L, SC_K, GROUP_W), SC_K ** -0.5),
        'pool_w': nrm(27, (L, POOL_G, POOL_CH, POOL_CH), POOL_CH ** -0.5),
        'pool_scale': 1.0 + nrm(28, (L, GROUP_W), 0.1),
        'w_out': nrm(29, (L, D_MODEL, D_MODEL), D_MODEL ** -0.5),
        'peer_wq': nrm(30, (L, D_MODEL, PEER_HEADS * PEER_QDIM), D_MODEL ** -0.5),
        'peer_k1': nrm(31, (L, PEER_HEADS, N_KEYS, PEER_QDIM // 2), (PEER_QDIM // 2) ** -0.5),
        'peer_k2': nrm(32, (L, PEER_HEADS, N_KEYS, PEER_QDIM // 2), (PEER_QDIM // 2) ** -0.5),
        'peer_u': nrm(33, (L, N_EXPERTS, D_MODEL), D_MODEL ** -0.5),
        'peer_v': nrm(34, (L, N_EXPERTS, D_MODEL), PEER_HEADS ** -0.5),
    }

def reference(x_prompt, x_sample, state_conformer, state_rwkv_shift, state_rwkv_wkv,
              state_shortconv, state_pool, norm1_g, norm2_g, final_norm_g, w_in,
              conf_dw_w, conf_dw_b, conf_ln_g, conf_ln_b, rwkv_mu, rwkv_w0, rwkv_w2,
              rwkv_a0, rwkv_a2, rwkv_g2, rwkv_k_k, rwkv_k_a, rwkv_r_k, rwkv_ln_g, rwkv_ln_b,
              sc_conv_w, pool_w, pool_scale, w_out, peer_wq, peer_k1, peer_k2, peer_u, peer_v):
    layer_weights = {
        'w_in': w_in, 'conf_dw_w': conf_dw_w, 'conf_dw_b': conf_dw_b,
        'conf_ln_g': conf_ln_g, 'conf_ln_b': conf_ln_b, 'rwkv_mu': rwkv_mu,
        'rwkv_w0': rwkv_w0, 'rwkv_w2': rwkv_w2, 'rwkv_a0': rwkv_a0, 'rwkv_a2': rwkv_a2,
        'rwkv_g2': rwkv_g2, 'rwkv_k_k': rwkv_k_k, 'rwkv_k_a': rwkv_k_a, 'rwkv_r_k': rwkv_r_k,
        'rwkv_ln_g': rwkv_ln_g, 'rwkv_ln_b': rwkv_ln_b, 'sc_conv_w': sc_conv_w,
        'pool_w': pool_w, 'pool_scale': pool_scale, 'w_out': w_out,
    }

    def run(x, states, start_pos):
        new_states = ([], [], [], [], [])
        for l in range(DEPTH):
            wl = {name: arr[l] for name, arr in layer_weights.items()}
            bufs = tuple(s[l] for s in states)
            y, nb = token_mixers(rmsnorm(x, norm1_g[l]), bufs, start_pos, wl)
            x = x + y.astype(x.dtype)
            x = x + peer_ffn(rmsnorm(x, norm2_g[l]), peer_wq[l], peer_k1[l], peer_k2[l],
                             peer_u[l], peer_v[l])
            for lst, s in zip(new_states, nb):
                lst.append(s)
        stacked = tuple(jnp.stack(lst, axis=0) for lst in new_states)
        return rmsnorm(x, final_norm_g), stacked

    dt = x_prompt.dtype
    zero_states = (
        jnp.zeros((DEPTH, BATCH, CONF_K - 1, GROUP_W), dt),
        jnp.zeros((DEPTH, BATCH, RWKV_COLS), dt),
        jnp.zeros((DEPTH, BATCH, RWKV_H, RWKV_HEAD, RWKV_HEAD), dt),
        jnp.zeros((DEPTH, BATCH, SC_K - 1, GROUP_W), dt),
        jnp.zeros((DEPTH, BATCH, POOL_BUF, GROUP_W), dt),
    )
    y_prompt, (conf_p, shift_p, wkv_p, sc_p, pool_p) = run(x_prompt, zero_states, 0)
    y_sample, (conf_s, shift_s, wkv_s, sc_s, pool_s) = run(
        x_sample, (state_conformer, state_rwkv_shift, state_rwkv_wkv, state_shortconv, state_pool),
        PAST_LEN)
    return (y_prompt, y_sample, conf_p, conf_s, shift_p, shift_s, wkv_p, wkv_s, sc_p, sc_s, pool_p, pool_s)


_drawn_inputs = setup_inputs


def setup_inputs(seed=0):
    import zlib

    import numpy as np

    out = dict(_drawn_inputs(seed))
    spreads = {}
    factors = {'conf_dw_b': 2.759, 'conf_ln_b': 5.009, 'rwkv_ln_g': 3.025, 'rwkv_ln_b': 11.585}
    for name, (base, spread) in spreads.items():
        noise = np.random.default_rng([zlib.crc32(name.encode()), seed]).standard_normal(out[name].shape)
        drawn = base * np.exp(spread * noise) if base else spread * noise
        out[name] = jnp.asarray(drawn.astype(out[name].dtype))
    for name, factor in factors.items():
        out[name] = (out[name] * factor).astype(out[name].dtype)
    return out
```

```python
from contextlib import ExitStack

import numpy as np

import concourse.bass as bass
from concourse import mybir

F32 = mybir.dt.float32
U32 = mybir.dt.uint32
ALU = mybir.AluOpType
ACT = mybir.ActivationFunctionType
AX = mybir.AxisListType

D = 1024
KT = D // 128
SEQ = 512
NS = 8
NT = SEQ + NS
TILES = SEQ // 128
GW = 256
CK = 31
SK = 3
PB = 15
NZ = 19
HEADS = 8
TOPK = 16
NEXP = 16384
CH = 64
NCH = SEQ // CH
LEVELS = 6
DECAY = float(np.exp(-0.5))
NEG = -3.4e38

Z_GLU, Z_GATE, Z_LORA, Z_K, Z_R, Z_V, Z_B, Z_C, Z_H, Z_D = 0, 2, 4, 5, 7, 9, 11, 13, 15, 17


def column_order():
    a, b = 2 * GW, 2 * GW + 896
    r = range(a, a + 256)
    wlo = range(a + 256, a + 288)
    k = range(a + 288, a + 544)
    v = range(a + 544, a + 800)
    alo = range(a + 800, a + 832)
    glo = range(a + 832, a + 896)
    out = list(range(0, a))
    for part in (wlo, alo, glo, k, r, v):
        out += part
    return np.array(out + list(range(b, b + 1024)))


COLUMNS = {}
_n = 0
for _name, _w in [("g1", 8), ("mu", 7), ("w0", 2), ("a0", 2), ("kk", 2), ("ka", 2), ("rk", 2), ("lng", 2),
                  ("lnb", 2), ("cw", 2 * CK), ("cb", 2), ("clg", 2), ("clb", 2), ("sw", 2 * SK), ("ps", 2)]:
    COLUMNS[_name] = (_n, _w)
    _n += _w
NCOL = _n

CONSTS = {}
_n = 0
for _name, _w in [("ident", 128), ("blk", 128), ("blk64", 128), ("all256", 128), ("gmask", 128),
                  ("levels", LEVELS * CH), ("scan", SEQ), ("invcnt", 32), ("iota", TOPK), ("sel", 64),
                  ("sel2", 8), ("hmask", 8), ("imask", 64)]:
    CONSTS[_name] = (_n, _w)
    _n += _w
NCONST = _n


def constants():
    p = np.arange(128)
    c = {}
    c["ident"] = np.eye(128)
    c["blk"] = (p[:, None] // 64 == p[None] // 64).astype(float)
    c["blk64"] = c["blk"] / 64
    c["all256"] = np.full((128, 128), 1 / 256)
    s, t = p % CH, np.arange(CH)
    c["gmask"] = np.concatenate([s[:, None] < t[None], s[:, None] <= t[None]], 1).astype(float)
    lv = np.zeros((128, LEVELS, CH))
    for i in range(LEVELS):
        b = 1 << i
        lv[:, i] = ((s[:, None] // (2 * b) == t[None] // (2 * b)) & (s[:, None] % (2 * b) < b)
                    & (t[None] % (2 * b) >= b))
    c["levels"] = lv.reshape(128, -1)
    c["scan"] = np.tile((np.arange(SEQ) % CH != 0).astype(float), (128, 1))
    cnt = np.zeros((128, 2, 16))
    for cc in range(2):
        for q in range(128):
            win = 2 << (2 * cc + q // 64)
            cnt[q, cc] = 1.0 / np.minimum(win, np.arange(16) + 1)
    c["invcnt"] = cnt.reshape(128, -1)
    c["iota"] = np.tile(np.arange(TOPK), (128, 1))
    c["sel"] = (p[:, None] == np.arange(64)[None] % 8).astype(float)
    c["sel2"] = (p[:, None] % 8 == np.arange(8)[None]).astype(float)
    c["hmask"] = (p[:, None] // 8 == np.arange(8)[None]).astype(float)
    c["imask"] = (p[:, None] % 64 == np.arange(64)[None]).astype(float)
    return np.concatenate([c[n].astype(np.float32) for n in CONSTS], 1)


RING = 8
ROW = 2 * D
LEAD = 2


def build(nc, a):
    ctx = ExitStack()
    with ctx:
        def sem(name):
            return ctx.enter_context(nc.semaphore(name))

        SIZE = 53200
        arena = ctx.enter_context(nc.sbuf_tensor("arena", [128, SIZE], F32))
        ps = ctx.enter_context(nc.psum_tensor("ps", [128, 8, 512], F32))
        top = [0]

        def at(off, *shape):
            n = int(np.prod(shape))
            assert off + n <= SIZE
            v = arena[:, off:off + n]
            names = "abcd"[:len(shape)]
            if len(shape) > 1:
                v = v.rearrange(f"p ({' '.join(names)}) -> p {' '.join(names)}",
                                **{names[i]: shape[i] for i in range(1, len(shape))})
            return v

        def take(*shape):
            off = top[0]
            top[0] += int(np.prod(shape))
            return off, at(off, *shape)

        _, x = take(TILES + 1, D)
        o_xn, xn = take(TILES + 1, D)
        _, hT = take(KT, NT)
        _, const = take(NCONST)
        _, cols = take(NCOL)
        _, rows = take(2, D)
        _, st = take(4, TILES + 1)
        _, extc = take(2, NS, CK)
        _, extp = take(2, NS, PB + 1)
        _, extq = take(2, NS, SK)
        _, wc = take(2, NCH)
        _, state = take(2, CH)
        _, tails = take(2, 30 + 15 + 2)
        o_z, z = take(NZ, NT)
        o_xs, xs = take(7, NT)
        _, wring = take(3, KT, 128)
        _, yT = take(8, NT)
        o_t, _ = take(12, 2 * NT)

        _, poolw = take(2, 128)
        _, carrier = take(2)
        carrier = carrier[0:1]

        def cst(name):
            o, w = CONSTS[name]
            return const[:, o:o + w]

        def col(name, i=0, n=1):
            o, w = COLUMNS[name]
            return cols[:, o + i:o + i + n]

        ident, blk, blk64, all256, gmask = (cst(n) for n in ("ident", "blk", "blk64", "all256", "gmask"))
        levels = cst("levels").rearrange("p (l t) -> p l t", t=CH)
        imask = cst("imask")

        sgw, cum, ee, ei, ex, kk, kp, tmp, bb, aa, gg, bonus = (at(o_t + i * 2 * NT, 2, NT) for i in range(12))
        loraw = at(o_t + 11 * 2 * NT, GW)
        lt = at(o_t + 4 * 2 * NT, NT)
        o_c = o_z + 7 * NT
        ar, bk, av = (at(o_c + i * 2048, 2, NCH, 2, CH) for i in range(3))
        gs = at(o_xn, 2 * NCH, 2, 128)
        tinv = at(o_z, 4 * NCH, CH)
        p1t = at(o_z + 2048, 2 * NCH, CH)
        tinvt = at(o_xs, 4 * NCH, CH)
        u_sb = at(o_t, 4 * NCH, CH)
        lm = at(o_t + 2048, 4 * NCH, CH)
        xx = at(o_t + 2 * 2048, 2 * NCH, 128)
        atok = at(o_t + 3 * 2048, 2 * NCH, 128)
        bktok = at(o_t + 4 * 2048, 2 * NCH, 128)
        p2 = u_sb
        mv = lm
        tmp_ln = at(o_t, 2, NT)
        assert 5 * 2048 <= 10 * 2 * NT and 3 * 2048 + 7 * NT <= NZ * NT
        gpad = at(o_xn, 2, CK - 1 + SEQ)
        cacc = at(o_xn + 1084, 2, NT)
        csq = at(o_xn + 2124, 2, NT)
        ctmp = at(o_xn + 3164, 2, NS, CK)
        ppad = at(o_xn, 2, PB + SEQ)
        pa = at(o_xn + 1054, 2, PB + SEQ)
        pb = at(o_xn + 2108, 2, PB + SEQ)
        pw = at(o_xn + 3162, 2, NT)
        qpad = at(o_xn, 2, SK - 1 + SEQ)
        cq = at(o_xn + 1100, 2, NT)
        qtmp = at(o_xn + 2300, 2, NS, SK)
        sst = at(o_xn + 4096, 2, NS, CH)
        sp = at(o_xn, 2, NS, CH)
        e = o_z
        ring = at(e, RING, ROW)
        e += RING * ROW
        wq = at(e, KT, 256)
        k12 = at(e + 2048, 2, 128)
        wqk = at(e, 2048 + 256)
        e += 2048 + 256
        diag = at(e, 4, 128)
        e += 512
        junk = at(e, 2, D)
        e += 2 * D
        xrep = at(e, D)
        e += D
        qT = at(e, 2, 128)
        e += 256
        qrep = at(e, 2, 64)
        e += 128
        sscore = at(e, 2, 128)
        e += 256
        v16 = at(e, 2, TOPK)
        e += 32
        i16 = at(e, 2 * TOPK).bitcast(U32).rearrange("p (a b) -> p a b", b=TOPK)
        e += 32
        i16f = at(e, 2, TOPK)
        e += 32
        scr = at(e, 256)
        e += 256
        cand = at(e, TOPK, TOPK)
        candf = at(e, 256)
        e += 256
        sc16 = at(e, TOPK)
        e += 16
        pos = at(e, TOPK).bitcast(U32)
        e += 16
        abu = at(e, 2 * TOPK).bitcast(U32)
        e += 32
        abf = at(e, 2 * TOPK)
        e += 32
        onehot = at(e, 2, TOPK, TOPK)
        scores = at(e, 256)
        e += 512
        ef = at(e, 2, TOPK)
        e += 32
        negm = at(e, 1)
        e += 1
        ssum = at(e, 2)
        e += 3
        idx = at(e, 5 * TOPK).bitcast(U32).rearrange("p (a b) -> p a b", b=TOPK)
        e += 80
        gate = at(e, 5, TOPK)
        e += 80
        hsel = at(e, 2, TOPK)
        e += 32
        gl = at(e, 2, TOPK)
        e += 32
        wgt = at(e, 2, TOPK)
        e += 32
        assert e <= o_t + 12 * 2 * NT

        d_const, d_cols, d_rows, d_small, d_out = (sem(n) for n in ("d_const", "d_cols", "d_rows", "d_small", "d_out"))
        d_x = [sem(f"d_x{t}") for t in range(TILES + 1)]
        d_w = [sem(f"d_w{i}") for i in range(3)]
        d_sst, d_wqk, d_shift, d_swkv = sem("d_sst"), sem("d_wqk"), sem("d_shift"), sem("d_swkv")
        d_row = [sem(f"d_row{i}") for i in range(RING)]
        act_chain, dve_chain = sem("act_chain"), sem("dve_chain")
        names = """sq_done mean_done root_done xn_done turned hT_done z_done z_copied zs_copied
            gate_done glu_done conf_sum conf_centered conf_sq conf_var conf_eps conf_root conf_u conf_sig
            xs_done lora_act lora_mm lora_out kk_sq kk_sum kk_max kk_root bonus_in bonus_sum
            cum_done exp_done pool_in pool_mm sample_in sample_mm composites
            turned_tok tok_copied g_mm g_masked lm_ready u_mm u_copied v_mm l1_mm
            mv_mm mv_copied p_mm p_copied sa_mm x_ready ys_mm y_copied state_ready
            ln_in ln_sum ln_root y_ready out_mm x1_done sq2 mean2 root2 xn2_done turned2 hT2_done
            wout_used tails_done samp_out
            xrep_mm xrep_done q_mm q_copied score_mm score_used exp_in exp2_done idx_ready
            dot_done gelu_done diag_done slot_used unit_mm unit_added sq_mm sq_copied ss_mm ss_added
            carried fin_sq fin_mean fin_root fin_done""".split()
        S = {n: sem(n) for n in names}
        dve_loop, weight_done = sem("dve_loop"), sem("weight_done")
        block = ctx.enter_context(nc.Block())

        def psv(b, n=512):
            return ps[:, b, 0:n]

        UNITS = HEADS * TILES
        OUT_CHUNKS = 8
        PAIRS = [0, 2, 3, 1]

        @block.sync
        def _(sp_):
            sp_.dma_start(const, a["const"][:, :]).then_inc(d_const, 16)
            sp_.dma_start(cols, a["cols"][:, :]).then_inc(d_cols, 16)
            for t in range(TILES):
                sp_.dma_start(x[:, t, :], a["xp"][128 * t:128 * t + 128, :]).then_inc(d_x[t], 16)
            sp_.dma_start(x[0:NS, TILES, :], a["xs"][:, :]).then_inc(d_x[TILES], 16)

            def weights(i, src):
                if 3 <= i < NZ + 3:
                    sp_.wait_ge(S["z_done"], i - 2)
                elif i >= NZ + 3:
                    m = i - NZ - 3
                    if m % 4 == 3:
                        sp_.wait_ge(S["out_mm"], (TILES + 1) * (m // 4 + 1))
                    else:
                        sp_.wait_ge(S["wout_used"], m + 1 - (m + 1) // 4)
                sp_.dma_start(wring[:, i % 3, :, :].rearrange("p a b -> p (a b)"), src).then_inc(d_w[i % 3], 16)

            for i in range(3):
                weights(i, a["win"][i])
            sp_.dma_start(extc[:, :, :, 0:CK - 1], a["sconf"][:, :, :, :]).then_inc(d_small, 16)
            sp_.dma_start(extp[:, :, :, 0:PB], a["spool"][:, :, :, :]).then_inc(d_small, 16)
            sp_.dma_start(extq[:, :, :, 0:SK - 1], a["ssc"][:, :, :, :]).then_inc(d_small, 16)
            sp_.dma_start(loraw, a["lora"][:, :]).then_inc(d_small, 16)
            sp_.dma_start(poolw, a["poolw"][:, :, :]).then_inc(d_small, 16)
            sp_.dma_start(yT[:, 0:7, 512:520], a["sshift"][:, :, :]).then_inc(d_small, 16)
            for i in range(3, 8):
                weights(i, a["win"][i])
            sp_.dma_start(rows[:, 0, :], a["n2"][0:1, :].partition_broadcast(128).rearrange("p a n -> p (a n)")).then_inc(d_rows, 16)
            sp_.dma_start(rows[:, 1, :], a["nf"][0:1, :].partition_broadcast(128).rearrange("p a n -> p (a n)")).then_inc(d_rows, 16)
            for i in range(8, NZ):
                weights(i, a["win"][i])
            sp_.wait_ge(S["zs_copied"], 2)
            sp_.wait_ge(S["z_copied"], Z_B)
            sp_.dma_start(a["o_shift"][:, :, :], z[:, Z_LORA:Z_B, SEQ - 1:NT]).then_inc(d_shift, 16)
            sp_.wait_ge(S["y_ready"], 3)
            sp_.dma_start(sst, a["swkv"][:, :, :, :]).then_inc(d_sst, 16)
            sp_.wait_ge(S["tails_done"], 3)
            sp_.dma_start(a["o_tails"][:, :], tails.rearrange("p a b -> p (a b)")).then_inc(d_out, 16)
            sp_.dma_start(a["o_sconf"][:, :, :, :], extc[:, :, :, 1:CK]).then_inc(d_out, 16)
            sp_.dma_start(a["o_spool"][:, :, :, :], extp[:, :, :, 1:PB + 1]).then_inc(d_out, 16)
            sp_.dma_start(a["o_ssc"][:, :, :, :], extq[:, :, :, 1:SK]).then_inc(d_out, 16)
            sp_.wait_ge(S["samp_out"], 1)
            sp_.dma_start(a["o_swkv"][:, :, :, :], sst).then_inc(d_swkv, 16)
            for i in range(OUT_CHUNKS):
                weights(NZ + i, a["wout"][i])
            sp_.wait_ge(S["state_ready"], NCH + 1)
            sp_.dma_start(a["o_wkv"][:, :, :], state).then_inc(d_out, 16)

            sp_.wait_ge(S["x1_done"], 2 * (TILES + 1))
            sp_.wait_ge(d_out, 16 * 5)
            sp_.wait_ge(d_shift, 16)
            sp_.wait_ge(d_swkv, 16)
            sp_.dma_start(wqk, a["wqk"][0]).then_inc(d_wqk, 16)
            with sp_.Fori(0, HEADS - 1) as h:
                sp_.wait_ge(S["score_mm"], TILES * (h + 1))
                sp_.wait_ge(S["ss_mm"], h + 1)
                sp_.dma_start(wqk, a["wqk"][bass.ds(h + 1, 1), :, :].rearrange("a p n -> (a p) n")).then_inc(d_wqk, 16)
            for t in range(TILES + 1):
                sp_.wait_ge(S["fin_done"], t + 1)
                if t < TILES:
                    sp_.dma_start(a["yp"][128 * t:128 * t + 128, :], xn[:, t, :]).then_inc(d_out, 16)
                else:
                    sp_.dma_start(a["ys"][:, :], xn[0:NS, TILES, :]).then_inc(d_out, 16)
            sp_.wait_ge(d_out, 16 * (5 + TILES + 1))

        @block.tensor
        def _(pe):
            mm, turn = nc.tensor.matmul, nc.tensor.transpose

            def transposes(ready, freed, out):
                for t in range(TILES + 1):
                    n = 128 if t < TILES else NS
                    pe.wait_ge(S[ready], t + 1)
                    if t >= 2:
                        pe.wait_ge(S[freed], t - 1)
                    for k in range(KT):
                        last = turn(ps[:, 4 + 2 * (t % 2) + k // 4, (k % 4) * 128:(k % 4) * 128 + n],
                                    xn[0:n, t, 128 * k:128 * k + 128], ident[0:n, 0:n])
                    last.then_inc(S[out], 1)

            def pairs(mat, src, banks, sbank, scol, joint=False):
                last = None
                for part in range(2):
                    for cc in range(2):
                        o = 0 if joint else cc
                        dst = ps[:, banks[o], :] if part == 0 else ps[:, sbank, scol + 8 * o:scol + 8 * o + 8]
                        s = src[:, cc, 0:SEQ] if part == 0 else src[:, cc, SEQ:NT]
                        last = mm(dst, mat, s, start=(cc == 0 or not joint), stop=(cc == 1 or not joint))
                return last

            pe.wait_ge(d_const, 16)
            transposes("xn_done", "hT_done", "turned")
            pe.wait_ge(S["hT_done"], TILES + 1)

            def project(i):
                pe.wait_ge(d_w[i % 3], 16 * (i // 3 + 1))
                if i >= 2:
                    pe.wait_ge(S["z_copied"], i - 1)
                group = 0 if i < Z_LORA else 1 if i < Z_B else 2
                base = (0, Z_LORA, Z_B)[group]
                if i == Z_B:
                    pe.wait_ge(S["zs_copied"], 1)
                for k in range(KT):
                    mm(ps[:, i % 2, :], wring[:, i % 3, k, :], hT[:, k, 0:SEQ], start=(k == 0), stop=(k == KT - 1))
                for k in range(KT):
                    last = mm(ps[:, 2 + group % 2, 8 * (i - base):8 * (i - base) + 8], wring[:, i % 3, k, :],
                              hT[:, k, SEQ:NT], start=(k == 0), stop=(k == KT - 1))
                last.then_inc(S["z_done"], 1)

            for i in range(Z_K):
                project(i)
            for i in range(Z_K, Z_B):
                project(i)
            pe.wait_ge(S["conf_sum"], 1)
            pairs(all256, cacc, [4], 5, 0, joint=True).then_inc(S["conf_centered"], 1)
            project(Z_B)
            pe.wait_ge(S["conf_sq"], 1)
            pairs(all256, csq, [6], 5, 8, joint=True).then_inc(S["conf_var"], 1)
            pe.wait_ge(S["lora_act"], 1)
            pe.wait_ge(d_small, 16 * 6)
            pe.wait_ge(S["conf_root"], 1)
            pe.wait_ge(S["zs_copied"], 2)
            for n, (lo, hi) in enumerate([(0, 32), (32, 64), (64, 128)]):
                if n:
                    project(Z_B + n)
                    pe.wait_ge(S["lora_out"], n)
                for cc in range(2):
                    w = loraw[lo:hi, 128 * cc:128 * cc + 128]
                    mm(ps[:, 4 + 2 * (n % 2) + cc, :], w, lt[lo:hi, 0:SEQ], start=True, stop=True)
                    last = mm(ps[:, 3, 128 + 16 * n + 8 * cc:136 + 16 * n + 8 * cc], w, lt[lo:hi, SEQ:NT],
                              start=True, stop=True)
                last.then_inc(S["lora_mm"], 1)
            pe.wait_ge(S["kk_sq"], 1)
            pe.wait_ge(S["lora_out"], 3)
            pairs(blk, tmp, [6, 7], 3, 192).then_inc(S["kk_sum"], 1)
            project(Z_C + 1)
            project(Z_H)
            pe.wait_ge(S["bonus_in"], 1)
            pairs(blk, tmp, [4, 5], 3, 224).then_inc(S["bonus_sum"], 1)
            for i in range(Z_H + 1, NZ):
                project(i)
            pe.wait_ge(S["pool_in"], 1)
            for cc in range(2):
                mm(ps[:, 6 + cc, :], poolw[:, cc, :], pw[:, cc, 0:SEQ], start=True, stop=True)
                last = mm(ps[:, 2, 256 + 8 * cc:264 + 8 * cc], poolw[:, cc, :], pw[:, cc, SEQ:NT], start=True, stop=True)
            last.then_inc(S["pool_mm"], 1)
            for n in range(3):
                pe.wait_ge(S["sample_in"], n + 1)
                if n == 0:
                    pe.wait_ge(S["bonus_in"], 2)
                for cc in range(2):
                    last = mm(ps[:, 4 + 2 * (n % 2) + cc, :], blk, sp[:, cc, :, :].rearrange("p a b -> p (a b)"),
                              start=True, stop=True)
                last.then_inc(S["sample_mm"], 1)

            pe.wait_ge(S["composites"], 1)
            for n in range(8):
                src = av if n < 4 else bk
                for j in range(4):
                    u = 4 * (n % 4) + j
                    if n == 0 and j == 0:
                        pe.wait_ge(S["z_copied"], NZ)
                    if n == 2 and j == 0:
                        pe.wait_ge(S["samp_out"], 1)
                    last = turn(ps[:, n, 128 * j:128 * j + 128],
                                src[:, u % 2, u // 2, :, :].rearrange("p a b -> p (a b)"), ident)
                last.then_inc(S["turned_tok"], 1)
            for n in range(4):
                pe.wait_ge(S["tok_copied"], 2 * n + 2)
                for j in range(4):
                    u = 4 * n + j
                    for par in range(2):
                        r = slice(64 * par, 64 * par + 64)
                        last = mm(ps[:, 2 * n + par, 128 * j:128 * j + 128],
                                  bk[r, u % 2, u // 2, :, :].rearrange("p a b -> p (a b)"),
                                  ar[r, u % 2, u // 2, :, :].rearrange("p a b -> p (a b)"), start=True, stop=True)
                        if j == 3:
                            last.then_inc(S["g_mm"], 1)

            def unit64(q):
                return range(8 * q, 8 * q + 8)

            for q in range(4):
                pe.wait_ge(S["lm_ready"], q + 1)
                for i in unit64(q):
                    last = mm(ps[0:64, 4 + q, 64 * (i % 8):64 * (i % 8) + 64], lm[0:64, i, :], ident[0:64, 0:64],
                              start=True, stop=True)
                last.then_inc(S["l1_mm"], 1)
            for lv in range(1, LEVELS):
                for q in range(4):
                    pe.wait_ge(S["lm_ready"], 4 * lv + q + 1)
                    for i in unit64(q):
                        last = mm(ps[0:64, q, 64 * (i % 8):64 * (i % 8) + 64], lm[0:64, i, :], tinv[0:64, i, :],
                                  start=True, stop=True)
                    last.then_inc(S["u_mm"], 1)
                for q in range(4):
                    pe.wait_ge(S["u_copied"], 4 * (lv - 1) + q + 1)
                    if lv < LEVELS - 1:
                        for i in unit64(q):
                            mm(ps[0:64, 4 + q, 64 * (i % 8):64 * (i % 8) + 64], tinvt[0:64, i, :], u_sb[0:64, i, :],
                               start=True, stop=True)
                    for i in unit64(q):
                        last = mm(ps[0:64, q, 64 * (i % 8):64 * (i % 8) + 64], u_sb[0:64, i, :], tinvt[0:64, i, :],
                                  start=True, stop=True)
                    last.then_inc(S["v_mm"], 1)
            for q in range(4):
                pe.wait_ge(S["lm_ready"], 4 * LEVELS + q + 1)
                for i in unit64(q):
                    last = mm(ps[0:64, q, 64 * (i % 8):64 * (i % 8) + 64], gs[64:128, i // 2, i % 2, 0:64],
                              xx[64:128, i // 2, 64 * (i % 2):64 * (i % 2) + 64], start=True, stop=True)
                last.then_inc(S["mv_mm"], 1)
            for q in range(4):
                pe.wait_ge(S["mv_copied"], q + 1)
                for i in unit64(q):
                    r = 64 * (i % 2)
                    mm(ps[r:r + 64, 4 + q, 64 * (i % 8 // 2):64 * (i % 8 // 2) + 64], atok[0:64, i // 2, r:r + 64],
                       tinvt[0:64, i, :], start=True, stop=True)
                for i in unit64(q):
                    last = mm(ps[0:64, q, 64 * (i % 8):64 * (i % 8) + 64], tinvt[0:64, i, :], mv[0:64, i, :],
                              start=True, stop=True)
                last.then_inc(S["p_mm"], 1)
            pe.wait_ge(S["p_copied"], 4)
            for c in range(NCH):
                pe.wait_ge(S["state_ready"], c + 1)
                b = c % 2
                for cc in range(2):
                    for par in range(2):
                        r = slice(64 * par, 64 * par + 64)
                        last = mm(ps[0:64, b + 6 * par, 64 * cc:64 * cc + 64], p1t[r, 2 * c + cc, :],
                                  state[r, cc, :], start=True, stop=True)
                last.then_inc(S["sa_mm"], 1)
                pe.wait_ge(S["x_ready"], 2 * c + 2)
                if c >= 2:
                    pe.wait_ge(S["y_copied"], c - 1)
                for cc in range(2):
                    for par in range(2):
                        r = slice(64 * par, 64 * par + 64)
                        i = xx[:, 2 * c + cc, 64 * par:64 * par + 64]
                        last = mm(ps[r, 4 + b, 64 * cc:64 * cc + 64], bktok[:, 2 * c + cc, 64 * par:64 * par + 64], i,
                                  start=True, stop=True)
                last.then_inc(S["ys_mm"], 1)
                for cc in range(2):
                    for par in range(2):
                        r = slice(64 * par, 64 * par + 64)
                        i = xx[:, 2 * c + cc, 64 * par:64 * par + 64]
                        mm(ps[r, 2 + b, 64 * cc:64 * cc + 64], state[r, cc, :], ar[r, cc, c, 1, :], start=True, stop=False)
                        last = mm(ps[r, 2 + b, 64 * cc:64 * cc + 64], i, gs[:, 2 * c + cc, par, 64:128],
                                  start=False, stop=True)
                last.then_inc(S["ys_mm"], 1)
            pe.wait_ge(S["y_copied"], NCH)
            pairs(blk64, yT[:, 2:4, :], [6, 7], 0, 0).then_inc(S["ln_sum"], 1)
            pe.wait_ge(S["ln_in"], 1)
            pairs(blk64, tmp_ln, [4, 5], 1, 0).then_inc(S["ln_sum"], 1)
            pe.wait_ge(S["y_ready"], 4)
            for i in range(OUT_CHUNKS):
                nh, pair = i // 4, PAIRS[i % 4]
                j = NZ + i
                pe.wait_ge(d_w[j % 3], 16 * (j // 3 + 1))
                w = wring[:, j % 3, :, :].rearrange("p a b -> p (a b)").rearrange("p (a b) -> p a b", b=512)
                for k in range(2):
                    for t in range(TILES + 1):
                        n = 128 if t < TILES else NS
                        if i == 4 and k == 0 and t >= 3:
                            pe.wait_ge(S["x1_done"], t - 2)
                        last = mm(ps[0:n, (5 * nh + t) % 8, :], yT[:, 2 * pair + k, 128 * t:128 * t + n], w[:, k, :],
                                  start=(i % 4 == 0 and k == 0), stop=(i % 4 == 3 and k == 1))
                        if i % 4 == 3 and k == 1:
                            last.then_inc(S["out_mm"], 1)
                if not (i % 4 == 3):
                    last.then_inc(S["wout_used"], 1)
            pe.wait_ge(S["x1_done"], 2 * (TILES + 1))
            transposes("xn2_done", "hT2_done", "turned2")
            pe.wait_ge(S["hT2_done"], TILES + 1)

            for n in range(2):
                last = mm(ps[0:64, n, :], cst("sel")[0:NS, :], xn[0:NS, TILES, 512 * n:512 * n + 512], start=True, stop=True)
            last.then_inc(S["xrep_mm"], 1)
            pe.wait_ge(S["xrep_done"], 1)

            def query(h, t):
                v = TILES * h + t
                if t == 0:
                    pe.wait_ge(d_wqk, 16 * (h + 1))
                if not (isinstance(h, int) and v == 0):
                    pe.wait_ge(S["q_copied"], v)
                for half in range(2):
                    for k in range(KT):
                        last = mm(ps[:, 4, 128 * half:128 * half + 128], wq[:, k, 128 * half:128 * half + 128],
                                  hT[:, k, 128 * t:128 * t + 128], start=(k == 0), stop=(k == KT - 1))
                last.then_inc(S["q_mm"], 1)

            def score(h, t):
                v = TILES * h + t
                pe.wait_ge(S["q_copied"], v + 1)
                if not (isinstance(h, int) and v == 0):
                    pe.wait_ge(S["score_used"], v)
                for half in range(2):
                    last = mm(ps[:, 5, 128 * half:128 * half + 128], qT[:, half, :], k12[:, half, :], start=True, stop=True)
                last.then_inc(S["score_mm"], 1)

            def sample_query(h):
                if not (isinstance(h, int) and h == 0):
                    pe.wait_ge(S["ss_added"], h)
                for half in range(2):
                    for k in range(KT):
                        last = mm(ps[:, 6, 256 + 8 * half:264 + 8 * half], wq[:, k, 128 * half:128 * half + 128],
                                  hT[:, k, SEQ:NT], start=(k == 0), stop=(k == KT - 1))
                last.then_inc(S["sq_mm"], 1)
                pe.wait_ge(S["sq_copied"], h + 1)
                for half in range(2):
                    last = mm(ps[0:64, 6, 128 * half:128 * half + 128], qrep[:, half, :], k12[:, half, :], start=True, stop=True)
                last.then_inc(S["ss_mm"], 1)

            def prepare(h, t, step):
                if step == 0:
                    query(h, t)
                else:
                    score(h, t)
                    if t == 0:
                        sample_query(h)

            def unit(h, t, nxt):
                u = TILES * h + t
                n = 128 if t < TILES else 64
                m = 128 if t < TILES else NS
                b = 2 * (t % 2)
                pe.wait_ge(S["unit_added"], u + 1)
                for s in range(TOPK):
                    pe.wait_ge(S["diag_done"], TOPK * u + s + 1)
                    for c in range(2):
                        last = mm(ps[0:m, b + c, :], diag[0:n, s % 4, 0:m], ring[0:n, s % RING, D + 512 * c:D + 512 * c + 512],
                                  start=(s == 0), stop=(s == TOPK - 1))
                    last.then_inc(S["slot_used"], 1)
                    if nxt and s in (3, 5):
                        prepare(nxt[0], nxt[1], 0 if s == 3 else 1)

            pe.sem_inc(S["slot_used"], RING)
            pe.sem_inc(S["unit_added"], 2)
            for t in range(LEAD):
                prepare(0, t, 0)
                prepare(0, t, 1)
            with pe.Fori(0, HEADS - 1) as h:
                for t in range(TILES):
                    unit(h, t, (h, t + LEAD) if t + LEAD < TILES else (h + 1, t + LEAD - TILES))
            for t in range(TILES):
                unit(HEADS - 1, t, (HEADS - 1, t + LEAD) if t + LEAD < TILES else None)
            unit(HEADS - 1, TILES, None)

        @block.scalar
        def _(act):
            f = nc.scalar.activation
            count = {}

            def link(ins, name=None):
                s = S[name] if name else act_chain
                count[name] = count.get(name, 0) + 1
                ins.then_inc(s, 1)
                act.wait_ge(s, count[name])

            def squares(t, ready, name, dst):
                n = 128 if t < TILES else NS
                f(dst[0:n, t, :], x[0:n, t, :], ACT.Square, accum_out=st[0:n, 0, t:t + 1]).then_inc(S[name], 1)

            def root(t, mean, name):
                n = 128 if t < TILES else NS
                act.wait_ge(S[mean], t + 1)
                f(st[0:n, 2, t:t + 1], st[0:n, 1, t:t + 1], ACT.Sqrt).then_inc(S[name], 1)

            act.wait_ge(d_const, 16)
            act.wait_ge(d_cols, 16)
            for t in range(TILES + 1):
                act.wait_ge(d_x[t], 16)
                squares(t, None, "sq_done", xn)
            for t in range(TILES + 1):
                root(t, "mean_done", "root_done")

            def copy_z(i):
                act.wait_ge(S["z_done"], i + 1)
                f(z[:, i, 0:SEQ], ps[:, i % 2, :], ACT.Copy).then_inc(S["z_copied"], 1)

            for i in range(Z_LORA):
                copy_z(i)
            act.wait_ge(S["zs_copied"], 1)
            act.wait_ge(S["z_copied"], Z_LORA)
            f(z[:, Z_GATE:Z_GATE + 2, :], z[:, Z_GATE:Z_GATE + 2, :], ACT.Sigmoid).then_inc(S["gate_done"], 1)
            for i in range(Z_LORA, Z_B):
                copy_z(i)
            copy_z(Z_B)
            act.wait_ge(S["xs_done"], 1)
            f(lt[0:32, :], xs[0:32, 0, :], ACT.Tanh)
            f(lt[32:64, :], xs[32:64, 0, :], ACT.Copy)
            f(lt[64:128, :], xs[64:128, 0, :], ACT.Sigmoid).then_inc(S["lora_act"], 1)
            act.wait_ge(S["conf_eps"], 1)
            f(csq, csq, ACT.Sqrt).then_inc(S["conf_root"], 1)

            def lora(n, dst, fun, bias):
                act.wait_ge(S["lora_mm"], n + 1)
                for cc in range(2):
                    kw = {"bias": col(bias, cc)} if bias else {}
                    f(dst[:, cc, 0:SEQ], ps[:, 4 + 2 * (n % 2) + cc, :], fun, **kw)
                    last = f(dst[:, cc, SEQ:NT], ps[:, 3, 128 + 16 * n + 8 * cc:136 + 16 * n + 8 * cc], fun, **kw)
                last.then_inc(S["lora_out"], 1)

            lora(0, sgw, ACT.Sigmoid, "w0")
            lora(1, aa, ACT.Sigmoid, "a0")
            copy_z(Z_B + 1)
            lora(2, gg, ACT.Copy, None)
            copy_z(Z_C)
            act.wait_ge(S["conf_u"], 1)
            f(csq, cacc, ACT.Sigmoid).then_inc(S["conf_sig"], 1)
            act.wait_ge(S["kk_max"], 1)
            f(tmp, tmp, ACT.Sqrt).then_inc(S["kk_root"], 1)
            copy_z(Z_C + 1)
            copy_z(Z_H)
            act.wait_ge(S["cum_done"], 1)
            f(ee[:, :, 0:SEQ], cum[:, :, 0:SEQ], ACT.Exp, scale=-DECAY)
            f(ei[:, :, 0:SEQ], cum[:, :, 0:SEQ], ACT.Exp, scale=DECAY)
            f(ex[:, :, 0:SEQ], ex[:, :, 0:SEQ], ACT.Exp, scale=-DECAY)
            f(cum[:, :, SEQ:NT], sgw[:, :, SEQ:NT], ACT.Exp, scale=-DECAY).then_inc(S["exp_done"], 1)
            for i in range(Z_H + 1, NZ):
                copy_z(i)

            for n in range(8):
                act.wait_ge(S["turned_tok"], n + 1)
                u = slice(4 * (n % 4), 4 * (n % 4) + 4)
                src = ps[:, n, :].rearrange("p (a b) -> p a b", b=128)
                if n < 4:
                    f(atok[0:64, u, :], src[0:64], ACT.Copy)
                    f(xx[64:128, u, :], src[64:128], ACT.Copy).then_inc(S["tok_copied"], 1)
                else:
                    f(bktok[:, u, :], src, ACT.Copy).then_inc(S["tok_copied"], 1)
            for lv in range(1, LEVELS):
                for q in range(4):
                    act.wait_ge(S["u_mm"], 4 * (lv - 1) + q + 1)
                    f(u_sb[0:64, 8 * q:8 * q + 8, :].rearrange("p a b -> p (a b)"), ps[0:64, q, :], ACT.Copy)\
                        .then_inc(S["u_copied"], 1)
            for q in range(4):
                act.wait_ge(S["mv_mm"], q + 1)
                f(mv[0:64, 8 * q:8 * q + 8, :].rearrange("p a b -> p (a b)"), ps[0:64, q, :], ACT.Copy)\
                    .then_inc(S["mv_copied"], 1)
            for q in range(4):
                act.wait_ge(S["p_mm"], q + 1)
                f(p1t[:, 4 * q:4 * q + 4, :].rearrange("p a b -> p (a b)"), ps[:, 4 + q, 0:256], ACT.Copy)
                f(p2[0:64, 8 * q:8 * q + 8, :].rearrange("p a b -> p (a b)"), ps[0:64, q, :], ACT.Copy)\
                    .then_inc(S["p_copied"], 1)
            for c in range(NCH):
                act.wait_ge(S["ys_mm"], 2 * c + 2)
                f(yT[:, 2:4, CH * c:CH * c + CH], ps[:, 2 + c % 2, 0:2 * CH].rearrange("p (a b) -> p a b", b=CH), ACT.Copy)\
                    .then_inc(S["y_copied"], 1)
            act.wait_ge(S["ln_in"], 2)
            f(tmp_ln, tmp_ln, ACT.Sqrt).then_inc(S["ln_root"], 1)

            for t in range(TILES + 1):
                act.wait_ge(S["x1_done"], TILES + 1 + t + 1)
                if t == 0:
                    act.wait_ge(S["hT_done"], TILES + 1)
                squares(t, None, "sq2", xn)
            for t in range(TILES + 1):
                root(t, "mean2", "root2")

            act.wait_ge(S["xrep_mm"], 1)
            for n in range(2):
                last = f(xrep[0:64, 512 * n:512 * n + 512], ps[0:64, n, :], ACT.Copy)
            last.then_inc(S["xrep_done"], 1)

            def queries(h, t):
                v = TILES * h + t
                act.wait_ge(S["q_mm"], v + 1)
                if not (isinstance(h, int) and v == 0):
                    act.wait_ge(S["score_mm"], v)
                f(qT.rearrange("p a b -> p (a b)"), ps[:, 4, 0:256], ACT.Copy).then_inc(S["q_copied"], 1)

            def sample_queries(h):
                if True:
                    act.wait_ge(S["sq_mm"], h + 1)
                    for half in range(2):
                        last = f(qrep[:, half, :].rearrange("p (a b) -> p a b", b=NS),
                                 ps[:, 6, 256 + 8 * half:264 + 8 * half].unsqueeze(1).to_broadcast([128, 8, NS]), ACT.Copy)
                    last.then_inc(S["sq_copied"], 1)

            def softmax(v, t):
                n = 128 if t < TILES else 64
                act.wait_ge(S["exp_in"], v + 1)
                f(gate[0:n, t, :], sc16[0:n, :], ACT.Exp, bias=negm[0:n, :], accum_out=ssum[0:n, 0:1]).then_inc(S["exp2_done"], 1)

            def unit(h, t, nxt):
                u = TILES * h + t
                n = 128 if t < TILES else 64
                b = t % 2
                for s in range(0, TOPK, 2):
                    act.wait_ge(S["dot_done"], TOPK * u + s + 2 + 2)
                    f(gl[0:n, b, s:s + 2], hsel[0:n, b, s:s + 2], ACT.Gelu).then_inc(S["gelu_done"], 1)
                    act.wait_ge(S["gelu_done"], (TOPK // 2) * u + s // 2 + 1)
                    for j in range(2):
                        last = f(wgt[0:n, b, s + j:s + j + 1], gl[0:n, b, s + j:s + j + 1], ACT.Copy,
                                 scale=gate[0:n, t, s + j:s + j + 1])
                    last.then_inc(weight_done, 1)
                    act.wait_ge(weight_done, (TOPK // 2) * u + s // 2 + 1)
                    for j in range(2):
                        act.wait_ge(S["slot_used"], TOPK * u + s + j - 3 + RING)
                        src = ident[0:n, :] if t < TILES else cst("sel2")[0:n, :]
                        f(diag[0:n, (s + j) % 4, 0:128 if t < TILES else NS], src, ACT.Copy,
                          scale=wgt[0:n, b, s + j:s + j + 1]).then_inc(S["diag_done"], 1)
                    if nxt and s == 2:
                        if nxt[1] < TILES:
                            queries(nxt[0], nxt[1])
                    if nxt and s == 6 and nxt[1] == 0:
                        sample_queries(nxt[0])
                    if nxt and s == TOPK - 4:
                        softmax(TILES * nxt[0] + nxt[1], nxt[1])

            act.wait_ge(S["hT2_done"], TILES + 1)
            for t in range(LEAD):
                queries(0, t)
                if t == 0:
                    sample_queries(0)
                softmax(t, t)
            with act.Fori(0, HEADS - 1) as h:
                for t in range(TILES):
                    unit(h, t, (h, t + LEAD) if t + LEAD < TILES else (h + 1, t + LEAD - TILES))

            def final(t):
                n = 128 if t < TILES else NS
                act.wait_ge(S["unit_added"], TILES * (HEADS - 1) + t + 1 + 2)
                f(xn[0:n, t, :], x[0:n, t, :], ACT.Square,
                  accum_out=st[0:n, 0, t:t + 1]).then_inc(S["fin_sq"], 1)
                act.wait_ge(S["fin_mean"], t + 1)
                f(st[0:n, 2, t:t + 1], st[0:n, 1, t:t + 1], ACT.Sqrt).then_inc(S["fin_root"], 1)

            last_h = HEADS - 1
            for t in range(TILES):
                nxt = (last_h, t + LEAD) if t + LEAD <= TILES else None
                unit(last_h, t, nxt)
            unit(last_h, TILES, None)
            for t in range(TILES + 1):
                final(t)

        @block.vector
        def _(dve):
            v = nc.vector
            count = {}

            def link(ins, name=None):
                s = S[name] if name else dve_chain
                count[name] = count.get(name, 0) + 1
                ins.then_inc(s, 1)
                dve.wait_ge(s, count[name])

            def tt(out, i0, i1, op):
                return v.tensor_tensor(out, i0, i1, op)

            def ts(out, i0, s1, op0, s2=None, op1=None):
                return v.tensor_scalar(out, i0, s1, s2, op0, op1) if op1 is not None else v.tensor_scalar(out, i0, s1, None, op0)

            def stt(out, i0, s, i1, op0, op1):
                return v.scalar_tensor_tensor(out=out, in0=i0, scalar=s, in1=i1, op0=op0, op1=op1)

            MUL, ADD, SUB, MAX = ALU.mult, ALU.add, ALU.subtract, ALU.max

            def features(t, turned, done, gain):
                n = 128 if t < TILES else NS
                dve.wait_ge(S[turned], t + 1)
                src = ps[:, 4 + 2 * (t % 2):6 + 2 * (t % 2), :].rearrange("p a (b c) -> p (a b) c", c=128)[:, :, 0:n]
                dst = hT[:, :, 128 * t:128 * t + n]
                if gain:
                    link(tt(dst, src, col("g1", 0, KT).unsqueeze(2).to_broadcast([128, KT, n]), MUL), done)
                else:
                    link(v.tensor_copy(dst, src), done)

            def mean(t, sq, name):
                n = 128 if t < TILES else NS
                dve.wait_ge(S[sq], t + 1)
                link(ts(st[0:n, 1, t:t + 1], st[0:n, 0, t:t + 1], 1.0 / D, MUL, 1e-6, ADD), name)

            link(v.memset(state, 0.0), "state_ready")
            dve.wait_ge(d_cols, 16)
            dve.wait_ge(d_const, 16)
            for t in range(TILES + 1):
                mean(t, "sq_done", "mean_done")
            for t in range(TILES + 1):
                n = 128 if t < TILES else NS
                dve.wait_ge(S["root_done"], t + 1)
                link(v.reciprocal(st[0:n, 3, t:t + 1], st[0:n, 2, t:t + 1]))
                link(ts(xn[0:n, t, :], x[0:n, t, :], st[0:n, 3, t:t + 1], MUL), "xn_done")
                if t >= 1:
                    features(t - 1, "turned", "hT_done", True)
            features(TILES, "turned", "hT_done", True)
            dve.wait_ge(d_small, 16 * 6)

            def sample_z(g):
                lo, hi = ((0, Z_LORA), (Z_LORA, Z_B), (Z_B, NZ))[g]
                dve.wait_ge(S["z_done"], hi)
                link(v.tensor_copy(z[:, lo:hi, SEQ:NT], ps[:, 2 + g % 2, 0:8 * (hi - lo)].rearrange("p (a b) -> p a b", b=8)),
                     "zs_copied")

            dve.wait_ge(S["turned"], TILES + 1)
            link(v.memset(gpad[:, :, 0:CK - 1], 0.0))
            sample_z(0)
            dve.wait_ge(S["gate_done"], 1)
            link(tt(gpad[:, :, CK - 1:], z[:, 0:2, 0:SEQ], z[:, 2:4, 0:SEQ], MUL))
            link(tt(extc[:, :, :, CK - 1], z[:, 0:2, SEQ:NT], z[:, 2:4, SEQ:NT], MUL))
            link(v.tensor_copy(tails[:, :, 0:30], gpad[:, :, SEQ:SEQ + 30]), "tails_done")
            cw = col("cw", 0, 2 * CK).rearrange("p (a b) -> p a b", b=CK)
            for k in range(CK):
                for cc in range(2):
                    o, i = cacc[:, cc, 0:SEQ], gpad[:, cc, k:k + SEQ]
                    w = cw[:, cc, k:k + 1]
                    ins = ts(o, i, w, MUL, col("cb", cc), ADD) if k == 0 else stt(o, i, w, o, MUL, ADD)
                    if cc == 0:
                        ins.then_inc(dve_chain, 1)
                        count[None] += 1
                    else:
                        link(ins)
            for cc in range(2):
                link(tt(ctmp[:, cc], extc[:, cc], cw[:, cc:cc + 1, :].to_broadcast([128, NS, CK]), MUL))
                link(v.tensor_reduce(cacc[:, cc, SEQ:NT], ctmp[:, cc], AX.X, ADD))
                link(ts(cacc[:, cc, SEQ:NT], cacc[:, cc, SEQ:NT], col("cb", cc), ADD), "conf_sum" if cc else None)
            sample_z(1)
            dve.wait_ge(S["z_copied"], Z_B)
            zr = z[:, Z_LORA:Z_B, :]
            link(tt(xs[:, :, 1:SEQ], zr[:, :, 0:SEQ - 1], zr[:, :, 1:SEQ], SUB))
            link(ts(xs[:, :, 0:1], zr[:, :, 0:1], -1.0, MUL))
            link(tt(xs[:, :, SEQ:NT], yT[:, 0:7, SEQ:NT], zr[:, :, SEQ:NT], SUB))
            for j in range(7):
                link(stt(xs[:, j, :], xs[:, j, :], col("mu", j), zr[:, j, :], MUL, ADD), "xs_done")
            dve.wait_ge(S["conf_centered"], 1)
            for cc in range(2):
                link(tt(cacc[:, cc, 0:SEQ], cacc[:, cc, 0:SEQ], ps[:, 4, :], SUB))
                link(tt(cacc[:, cc, SEQ:NT], cacc[:, cc, SEQ:NT], ps[:, 5, 0:8], SUB))
            link(tt(csq, cacc, cacc, MUL), "conf_sq")
            dve.wait_ge(S["conf_var"], 1)
            for cc in range(2):
                link(ts(csq[:, cc, 0:SEQ], ps[:, 6, :], 1e-5, ADD))
                link(ts(csq[:, cc, SEQ:NT], ps[:, 5, 8:16], 1e-5, ADD), "conf_eps" if cc else None)
            dve.wait_ge(S["conf_root"], 1)
            link(v.reciprocal(csq, csq))
            link(tt(cacc, cacc, csq, MUL))
            for cc in range(2):
                link(ts(cacc[:, cc, :], cacc[:, cc, :], col("clg", cc), MUL, col("clb", cc), ADD), "conf_u" if cc else None)

            lo_, k_, r_, v_ = xs[:, 0], xs[:, 1:3], xs[:, 3:5], xs[:, 5:7]
            for cc in range(2):
                link(ts(kk[:, cc, :], k_[:, cc, :], col("kk", cc), MUL))
            link(tt(tmp, kk, kk, MUL), "kk_sq")
            dve.wait_ge(S["lora_out"], 2)
            for cc in range(2):
                link(ts(kp[:, cc, :], aa[:, cc, :], -1.0, ADD, col("ka", cc), MUL))
                link(stt(kp[:, cc, :], kp[:, cc, :], 1.0, k_[:, cc, :], ADD, MUL))
            for cc in range(2):
                link(v.tensor_tensor_scan(cum[:, cc, 0:SEQ], cst("scan"), sgw[:, cc, 0:SEQ], 0.0, MUL, ADD))
            dve.wait_ge(S["lora_mm"], 3)
            link(tt(ex[:, :, 0:SEQ], cum[:, :, 0:SEQ], sgw[:, :, 0:SEQ], SUB), "cum_done")
            dve.wait_ge(S["kk_sum"], 1)
            link(ts(tmp[:, :, 0:SEQ], ps[:, 6:8, :], 1e-24, MAX))
            link(ts(tmp[:, :, SEQ:NT], ps[:, 3, 192:208].rearrange("p (a b) -> p a b", b=8), 1e-24, MAX), "kk_max")
            dve.wait_ge(S["conf_sig"], 1)
            link(tt(yT[:, 0:2, :], cacc, csq, MUL), "y_ready")
            dve.wait_ge(S["kk_root"], 1)
            link(v.reciprocal(tmp, tmp))
            link(tt(kk, kk, tmp, MUL))
            link(tt(bb, kk, aa, MUL))
            for cc in range(2):
                link(stt(tmp[:, cc, :], r_[:, cc, :], col("rk", cc), kp[:, cc, :], MUL, MUL), "bonus_in" if cc else None)
            sample_z(2)
            dve.wait_ge(S["z_copied"], NZ)
            dve.wait_ge(S["bonus_sum"], 1)
            link(tt(bonus[:, :, 0:SEQ], ps[:, 4:6, :], v_[:, :, 0:SEQ], MUL))
            link(tt(bonus[:, :, SEQ:NT], ps[:, 3, 224:240].rearrange("p (a b) -> p a b", b=8), v_[:, :, SEQ:NT], MUL), "bonus_in")
            W = PB + SEQ
            link(v.memset(ppad[:, :, 0:PB], 0.0))
            link(v.tensor_copy(ppad[:, :, PB:], z[:, Z_D:Z_D + 2, 0:SEQ]))
            link(v.tensor_copy(extp[:, :, :, PB], z[:, Z_D:Z_D + 2, SEQ:NT]))
            link(v.tensor_copy(tails[:, :, 30:45], ppad[:, :, SEQ:SEQ + PB]), "tails_done")
            src, lost = ppad, 0
            for lv, dst in enumerate((pa, pb, pa, pb)):
                sh = 1 << lv
                lost += sh
                link(tt(dst[:, :, lost:W], src[:, :, lost:W], src[:, :, lost - sh:W - sh], ADD))
                r = slice(64 * (lv % 2), 64 * (lv % 2) + 64)
                cc, win = lv // 2, 2 << lv
                inv = cst("invcnt").rearrange("p (a b) -> p a b", b=16)
                link(tt(pw[r, cc, 0:16], dst[r, cc, PB:PB + 16], inv[r, cc, :], MUL))
                link(ts(pw[r, cc, 16:SEQ], dst[r, cc, PB + 16:W], 1.0 / win, MUL))
                link(v.tensor_reduce(pw[r, cc, SEQ:NT], extp[r, cc, :, PB + 1 - win:PB + 1], AX.X, ADD))
                link(ts(pw[r, cc, SEQ:NT], pw[r, cc, SEQ:NT], 1.0 / win, MUL))
                src = dst
            link(tt(pw, pw, z[:, Z_D:Z_D + 2, :], SUB), "pool_in")
            dve.wait_ge(S["pool_mm"], 1)
            for cc in range(2):
                link(ts(yT[:, 6 + cc, 0:SEQ], ps[:, 6 + cc, :], col("ps", cc), MUL))
                link(ts(yT[:, 6 + cc, SEQ:NT], ps[:, 2, 256 + 8 * cc:264 + 8 * cc], col("ps", cc), MUL), "y_ready" if cc else None)
            link(v.memset(qpad[:, :, 0:SK - 1], 0.0))
            link(tt(qpad[:, :, SK - 1:], z[:, Z_C:Z_C + 2, 0:SEQ], z[:, Z_H:Z_H + 2, 0:SEQ], MUL))
            link(tt(extq[:, :, :, SK - 1], z[:, Z_C:Z_C + 2, SEQ:NT], z[:, Z_H:Z_H + 2, SEQ:NT], MUL))
            link(v.tensor_copy(tails[:, :, 45:47], qpad[:, :, SEQ:SEQ + 2]), "tails_done")
            sw = col("sw", 0, 2 * SK).rearrange("p (a b) -> p a b", b=SK)
            for cc in range(2):
                for k in range(SK):
                    o, i, w = cq[:, cc, 0:SEQ], qpad[:, cc, k:k + SEQ], sw[:, cc, k:k + 1]
                    link(ts(o, i, w, MUL) if k == 0 else stt(o, i, w, o, MUL, ADD))
                link(tt(qtmp[:, cc], extq[:, cc], sw[:, cc:cc + 1, :].to_broadcast([128, NS, SK]), MUL))
                link(v.tensor_reduce(cq[:, cc, SEQ:NT], qtmp[:, cc], AX.X, ADD))
            link(tt(yT[:, 4:6, :], cq, z[:, Z_B:Z_B + 2, :], MUL), "y_ready")

            def over_values(src):
                return src[:, :, SEQ:NT].unsqueeze(3).to_broadcast([128, 2, NS, CH])

            def spread(b):
                return ps[:, b:b + 2, :].rearrange("p a (b c) -> p a b c", c=CH)

            dve.wait_ge(d_sst, 16)
            dve.wait_ge(S["exp_done"], 1)
            link(tt(sp, sst, over_values(kk), MUL), "sample_in")
            link(tt(sst, sst, over_values(cum), MUL))
            dve.wait_ge(S["sample_mm"], 1)
            link(tt(sp, spread(4), over_values(bb), MUL))
            link(tt(sst, sst, sp, SUB))
            for cc in range(2):
                link(tt(sp[:, cc], imask.unsqueeze(1).to_broadcast([128, NS, CH]),
                        v_[:, cc, SEQ:NT].unsqueeze(2).to_broadcast([128, NS, CH]), MUL), "sample_in" if cc else None)
            dve.wait_ge(S["sample_mm"], 2)
            link(tt(sp, spread(6), over_values(kp), MUL))
            link(tt(sst, sst, sp, ADD))
            link(tt(sp, sst, over_values(r_), MUL), "sample_in")
            dve.wait_ge(S["sample_mm"], 3)
            for cc in range(2):
                link(tt(sp[:, cc], ps[:, 4 + cc, :].rearrange("p (b c) -> p b c", c=CH),
                        imask.unsqueeze(1).to_broadcast([128, NS, CH]), MUL))
                link(v.tensor_reduce(yT[:, 2 + cc, SEQ:NT], sp[:, cc], AX.X, ADD), "samp_out" if cc else None)

            dve.wait_ge(d_shift, 16)
            def chunks(src, cc):
                return src[:, cc, 0:SEQ].rearrange("p (n t) -> p n t", t=CH)

            for cc in range(2):
                link(stt(ar[:, cc, :, 0, :], chunks(kk, cc), -1.0, chunks(ex, cc), MUL, MUL))
                link(stt(av[:, cc, :, 0, :], chunks(kk, cc), -1.0, chunks(ex, cc), MUL, MUL))
                link(v.tensor_copy(av[:, cc, :, 1, :], chunks(v_, cc)))
                link(tt(ar[:, cc, :, 1, :], chunks(r_, cc), chunks(ee, cc), MUL))
                link(tt(bk[:, cc, :, 0, :], chunks(bb, cc), chunks(ei, cc), MUL))
                link(tt(bk[:, cc, :, 1, :], chunks(kp, cc), chunks(ei, cc), MUL))
                link(v.tensor_copy(wc[:, cc, :], chunks(ee, cc)[:, :, CH - 1]), "composites" if cc else None)
            for n in range(8):
                dve.wait_ge(S["g_mm"], n + 1)
                link(tt(gs[:, 4 * (n // 2):4 * (n // 2) + 4, n % 2, :],
                        ps[:, n, :].rearrange("p (a c) -> p a c", c=128),
                        gmask.unsqueeze(1).to_broadcast([128, 4, 128]), MUL), "g_masked")

            def lt_level(q, lv, name):
                g = gs[0:64, 4 * q:4 * q + 4, :, 0:64].rearrange("p a b c -> p (a b) c")
                m = levels[0:64, lv:lv + 1, :].to_broadcast([64, 8, CH])
                link(tt(lm[0:64, 8 * q:8 * q + 8, :], g, m, MUL), name)

            eye = ident[0:64, 0:64].unsqueeze(1).to_broadcast([64, 8, CH])
            for q in range(4):
                s = slice(8 * q, 8 * q + 8)
                lt_level(q, 0, "lm_ready")
                link(tt(tinvt[0:64, s, :], lm[0:64, s, :], eye, ADD))
            for q in range(4):
                s = slice(8 * q, 8 * q + 8)
                dve.wait_ge(S["l1_mm"], q + 1)
                link(tt(tinv[0:64, s, :], ps[0:64, 4 + q, :].rearrange("p (a b) -> p a b", b=CH), eye, ADD))
                lt_level(q, 1, "lm_ready")
            for lv in range(1, LEVELS):
                for q in range(4):
                    s = slice(8 * q, 8 * q + 8)
                    dve.wait_ge(S["v_mm"], 4 * (lv - 1) + q + 1)
                    last = lv == LEVELS - 1
                    if not last:
                        link(tt(tinv[0:64, s, :], tinv[0:64, s, :], ps[0:64, 4 + q, :].rearrange("p (a b) -> p a b", b=CH), ADD))
                    link(tt(tinvt[0:64, s, :], tinvt[0:64, s, :], ps[0:64, q, :].rearrange("p (a b) -> p a b", b=CH), ADD),
                         "lm_ready" if last else None)
                    if not last:
                        lt_level(q, lv + 1, "lm_ready")
            for c in range(NCH):
                dve.wait_ge(S["sa_mm"], c + 1)
                if c == 0:
                    dve.wait_ge(S["p_copied"], 4)
                for par in range(2):
                    link(tt(xx[0:64, 2 * c:2 * c + 2, 64 * par:64 * par + 64],
                            ps[0:64, c % 2 + 6 * par, 0:2 * CH].rearrange("p (a b) -> p a b", b=CH),
                            p2[0:64, 4 * c:4 * c + 4, :].rearrange("p (a b) c -> p a b c", b=2)[:, :, par, :], ADD), "x_ready")
                dve.wait_ge(S["ys_mm"], 2 * c + 2)
                link(tt(state, ps[:, 4 + c % 2, 0:2 * CH].rearrange("p (a b) -> p a b", b=CH), state, ADD))
                link(tt(state, state, wc[:, :, c].unsqueeze(2).to_broadcast([128, 2, CH]), MUL), "state_ready")
            yb = yT[:, 2:4, :]
            dve.wait_ge(S["y_copied"], NCH)
            dve.wait_ge(S["ln_sum"], 1)
            link(tt(yb[:, :, 0:SEQ], yb[:, :, 0:SEQ], ps[:, 6:8, :], SUB))
            link(tt(yb[:, :, SEQ:NT], yb[:, :, SEQ:NT], ps[:, 0, 0:16].rearrange("p (a b) -> p a b", b=8), SUB))
            link(tt(tmp_ln, yb, yb, MUL), "ln_in")
            dve.wait_ge(S["ln_sum"], 2)
            link(ts(tmp_ln[:, :, 0:SEQ], ps[:, 4:6, :], 64e-5, ADD))
            link(ts(tmp_ln[:, :, SEQ:NT], ps[:, 1, 0:16].rearrange("p (a b) -> p a b", b=8), 64e-5, ADD), "ln_in")
            dve.wait_ge(S["ln_root"], 1)
            link(v.reciprocal(tmp_ln, tmp_ln))
            link(tt(yb, yb, tmp_ln, MUL))
            for cc in range(2):
                link(ts(yb[:, cc, :], yb[:, cc, :], col("lng", cc), MUL, col("lnb", cc), ADD))
            link(tt(yb, yb, bonus, ADD))
            link(tt(yb, yb, gg, MUL), "y_ready")
            for nh in range(2):
                for t in range(TILES + 1):
                    n = 128 if t < TILES else NS
                    dve.wait_ge(S["out_mm"], 5 * nh + t + 1)
                    h = slice(512 * nh, 512 * nh + 512)
                    link(tt(x[0:n, t, h], x[0:n, t, h], ps[0:n, (5 * nh + t) % 8, :], ADD), "x1_done")
            for t in range(TILES + 1):
                mean(t, "sq2", "mean2")
            dve.wait_ge(d_rows, 32)
            dve.wait_ge(d_swkv, 16)
            for t in range(TILES + 1):
                n = 128 if t < TILES else NS
                dve.wait_ge(S["root2"], t + 1)
                link(v.reciprocal(st[0:n, 3, t:t + 1], st[0:n, 2, t:t + 1]))
                link(stt(xn[0:n, t, :], x[0:n, t, :], st[0:n, 3, t:t + 1], rows[0:n, 0, :], MUL, MUL), "xn2_done")
                if t >= 1:
                    features(t - 1, "turned2", "hT2_done", False)
            features(TILES, "turned2", "hT2_done", False)

            chain = [0]

            def loop_link(ins, base):
                chain[0] += 1
                v.drain()

            def choose(w, t, base, piece):
                n = 128 if t < TILES else 64

                def lk(ins):
                    loop_link(ins, base)

                if piece in (0, 1):
                    half = piece
                    if t < TILES:
                        if half == 0:
                            dve.wait_ge(S["score_mm"], w + 1)
                            lk(v.tensor_copy(scores[0:n], ps[0:n, 5, 0:256]))
                        sc = scores[0:n, 128 * half:128 * half + 128]
                    else:
                        sc = sscore[0:n, half, :]
                    a8, b8 = v16[0:n, half, 0:8], v16[0:n, half, 8:16]
                    lk(v.max(a8, sc))
                    lk(v.max_index(i16[0:n, half, 0:8], a8, sc))
                    lk(v.match_replace(scr[0:n, 0:128], a8, sc, NEG))
                    lk(v.max(b8, scr[0:n, 0:128]))
                    ins = v.max_index(i16[0:n, half, 8:16], b8, scr[0:n, 0:128])
                    lk(ins)
                    if half == 1 and t < TILES:
                        ins = ts(i16f[0:n, 0, :], i16[0:n, 0, :], 128.0, MUL)
                        ins.then_inc(S["score_used"], 1)
                        dve.wait_ge(S["score_used"], w + 1)
                    elif half == 1:
                        lk(ts(i16f[0:n, 0, :], i16[0:n, 0, :], 128.0, MUL))
                elif piece == 2:
                    lk(v.tensor_copy(i16f[0:n, 1, :], i16[0:n, 1, :]))
                    lk(tt(cand[0:n], v16[0:n, 0, :].unsqueeze(2).to_broadcast([n, TOPK, TOPK]),
                          v16[0:n, 1, :].unsqueeze(1).to_broadcast([n, TOPK, TOPK]), ADD))
                    lk(v.max(sc16[0:n, 0:8], candf[0:n]))
                    lk(v.max_index(pos[0:n, 0:8], sc16[0:n, 0:8], candf[0:n]))
                    lk(v.match_replace(scr[0:n], sc16[0:n, 0:8], candf[0:n], NEG))
                elif piece == 3:
                    lk(v.max(sc16[0:n, 8:16], scr[0:n]))
                    lk(v.max_index(pos[0:n, 8:16], sc16[0:n, 8:16], scr[0:n]))
                    ts(negm[0:n], sc16[0:n, 0:1], -1.0, MUL).then_inc(S["exp_in"], 1)
                    lk(v.tensor_single_scalar(abu[0:n, 0:16], pos[0:n], 4, ALU.logical_shift_right))
                    lk(v.tensor_single_scalar(abu[0:n, 16:32], pos[0:n], 15, ALU.bitwise_and))
                    lk(v.tensor_copy(abf[0:n], abu[0:n]))
                    oh = onehot[0:n].rearrange("p a b c -> p (a b) c")
                    lk(tt(oh, abf[0:n].unsqueeze(2).to_broadcast([n, 32, TOPK]),
                          cst("iota")[0:n].unsqueeze(1).to_broadcast([n, 32, TOPK]), ALU.is_equal))
                else:
                    lk(tt(onehot[0:n], onehot[0:n], i16f[0:n].unsqueeze(2).to_broadcast([n, 2, TOPK, TOPK]), MUL))
                    lk(v.tensor_reduce(ef[0:n], onehot[0:n], AX.X, ADD))
                    dve.wait_ge(S["exp2_done"], w + 1)
                    lk(v.reciprocal(ssum[0:n, 1:2], ssum[0:n, 0:1]))
                    lk(ts(gate[0:n, t, :], gate[0:n, t, :], ssum[0:n, 1:2], MUL))
                    tt(idx[0:n, t, :], ef[0:n, 0, :], ef[0:n, 1, :], ADD).then_inc(S["idx_ready"], 1)

            def sample_scores(h):
                dve.wait_ge(S["ss_mm"], h + 1)
                m = cst("hmask")[0:64, bass.ds(h, 1)] if not isinstance(h, int) else cst("hmask")[0:64, h:h + 1]
                flat = sscore[0:64].rearrange("p a b -> p (a b)")
                stt(flat, ps[0:64, 6, 0:256], m, flat, MUL, ADD).then_inc(S["ss_added"], 1)
                dve.wait_ge(S["ss_added"], h + 1)

            def unit(h, t, nxt, base):
                u = TILES * h + t
                n = 128 if t < TILES else 64
                row = xn[:, t, :] if t < TILES else xrep
                for s in range(TOPK):
                    dve.wait_ge(d_row[s % RING], 16 * (2 * u + s // RING + 1))
                    dve.wait_ge(S["dot_done"], TOPK * u + s + 1)
                    v.tensor_tensor_reduce(out=junk[0:n, s % 2], in0=ring[0:n, s % RING, 0:D], in1=row[0:n], scale=1.0, scalar=0.0,
                                           op0=MUL, op1=ADD, accum_out=hsel[0:n, t % 2, s:s + 1]).then_inc(S["dot_done"], 1)
                    if nxt:
                        if s == 7 and nxt[1] == 0:
                            sample_scores(nxt[0])
                        if s in (6, 8, 9, 11, 15):
                            choose(TILES * nxt[0] + nxt[1], nxt[1], base, (6, 8, 9, 11, 15).index(s))
                    if s == 3 and t:
                        add_unit(u - 1, t - 1)

            def add_unit(u, t):
                b = 2 * (t % 2)
                m = 128 if t < TILES else NS
                dve.wait_ge(S["slot_used"], TOPK * (u + 1) + RING)
                tt(x[0:m, t, :], x[0:m, t, :], ps[0:m, b:b + 2, :].rearrange("p a b -> p (a b)"), ADD)\
                    .then_inc(S["unit_added"], 1)

            dve.sem_inc(S["dot_done"], 2)
            link(v.memset(sscore[0:64], 0.0))
            for t in range(LEAD):
                for piece in range(5):
                    if piece == 3 and t == 0:
                        sample_scores(0)
                    choose(t, t, 0, piece)
            first = chain[0]
            per_choice = first // LEAD
            per_head = per_choice * TILES
            with dve.Fori(0, HEADS - 1) as h:
                chain[0] = 0
                for t in range(TILES):
                    nxt = (h, t + LEAD) if t + LEAD < TILES else (h + 1, t + LEAD - TILES)
                    unit(h, t, nxt, first + h * per_head)
                add_unit(TILES * h + TILES - 1, TILES - 1)
                assert chain[0] == per_head
            last_h = HEADS - 1
            chain[0] = 0
            for t in range(TILES):
                nxt = (last_h, t + LEAD) if t + LEAD <= TILES else None
                unit(last_h, t, nxt, first + last_h * per_head)
            unit(last_h, TILES, None, 0)
            add_unit(TILES * HEADS, TILES)
            for t in range(TILES + 1):
                n = 128 if t < TILES else NS
                mean(t, "fin_sq", "fin_mean")
                dve.wait_ge(S["fin_root"], t + 1)
                link(v.reciprocal(st[0:n, 3, t:t + 1], st[0:n, 2, t:t + 1]))
                link(stt(xn[0:n, t, :], x[0:n, t, :], st[0:n, 3, t:t + 1], rows[0:n, 1, :], MUL, MUL), "fin_done")

        @block.gpsimd
        def _(pool):
            pool.memset(carrier, 0.0).then_inc(S["carried"], 1)
            def gathers(h, t):
                u = TILES * h + t
                n = 128 if t < TILES else 64
                pool.wait_ge(S["idx_ready"], u + 1)
                for s in range(TOPK):
                    if s % 2 == 0:
                        pool.wait_ge(S["slot_used"], TOPK * u + s + 2)
                        pool.wait_ge(S["carried"], TOPK // 2 * u + s // 2 + 1)
                        pool.tensor_tensor(carrier[:, 1:2], carrier[:, 0:1], carrier[:, 0:1], ALU.add).then_inc(S["carried"], 1)
                    pool.indirect_dma_start(
                        out=ring[0:n, s % RING, :], out_offset=None, in_=a["uv"][:, :],
                        in_offset=bass.IndirectOffsetOnAxis(ap=idx[0:n, t, s:s + 1], axis=0),
                    ).then_inc(d_row[s % RING], 16)

            with pool.Fori(0, HEADS) as h:
                for t in range(TILES):
                    gathers(h, t)
            gathers(HEADS - 1, TILES)


def kernel(**inputs):
    import concourse.bacc as bacc
    from concourse.bass_utils import run_bass_kernel_spmd as run

    i = {k: np.asarray(v) for k, v in inputs.items()}
    order = column_order()

    def chans(v, lead=()):
        return np.asarray(v).reshape(-1, 128).T

    def per_chunk(v):
        v = np.moveaxis(v, -1, 0)
        return np.ascontiguousarray(v.reshape((-1, 128) + v.shape[1:]).swapaxes(0, 1))

    rw = order[512:512 + 896] - 512
    packed = {
        "g1": chans(i["norm1_g"][0]), "mu": chans(i["rwkv_mu"][0][rw]), "w0": chans(i["rwkv_w0"][0]),
        "a0": chans(i["rwkv_a0"][0]), "kk": chans(i["rwkv_k_k"][0]), "ka": chans(i["rwkv_k_a"][0]),
        "rk": chans(i["rwkv_r_k"][0].reshape(-1)), "lng": chans(i["rwkv_ln_g"][0]), "lnb": chans(i["rwkv_ln_b"][0]),
        "cw": per_chunk(i["conf_dw_w"][0]).reshape(128, -1), "cb": chans(i["conf_dw_b"][0]),
        "clg": chans(i["conf_ln_g"][0]), "clb": chans(i["conf_ln_b"][0]),
        "sw": per_chunk(i["sc_conv_w"][0]).reshape(128, -1), "ps": chans(i["pool_scale"][0]),
    }
    poolw = np.zeros((128, 2, 128), np.float32)
    for g in range(4):
        p = 64 * (g % 2)
        poolw[p:p + 64, g // 2, p:p + 64] = i["pool_w"][0, g]
    wout = i["w_out"][0].reshape(4, 2, 128, 2, 512)
    wqk = np.concatenate([
        i["peer_wq"][0].reshape(8, 128, HEADS, 256).transpose(2, 1, 0, 3).reshape(HEADS, 128, -1),
        i["peer_k1"][0].transpose(0, 2, 1), i["peer_k2"][0].transpose(0, 2, 1)], -1)
    wkv = i["state_rwkv_wkv"][0].reshape(NS, 2, 2, 64, 64)
    arrays = {
        "const": constants(),
        "cols": np.concatenate([packed[n] for n in COLUMNS], 1),
        "xp": i["x_prompt"][0], "xs": i["x_sample"][:, 0],
        "win": i["w_in"][0][:, order].reshape(KT, 128, NZ, 128).transpose(2, 1, 0, 3).reshape(NZ, 128, -1),
        "wout": np.stack([wout[p, :, :, h].transpose(1, 0, 2).reshape(128, -1) for h in range(2) for p in (0, 2, 3, 1)]),
        "wqk": wqk,
        "uv": np.concatenate([i["peer_u"][0], i["peer_v"][0]], 1),
        "n2": i["norm2_g"], "nf": i["final_norm_g"][None],
        "sconf": per_chunk(i["state_conformer"][0]), "spool": per_chunk(i["state_pool"][0]),
        "ssc": per_chunk(i["state_shortconv"][0]), "sshift": per_chunk(i["state_rwkv_shift"][0][:, rw]),
        "lora": np.concatenate([i["rwkv_w2"][0], i["rwkv_a2"][0], i["rwkv_g2"][0]], 0),
        "poolw": poolw,
        "swkv": wkv.transpose(2, 4, 1, 0, 3).reshape(128, 2, NS, 64),
    }
    outs = {
        "yp": (SEQ, D), "ys": (NS, D), "o_shift": (128, 7, 9), "o_tails": (128, 2 * 47),
        "o_sconf": (128, 2, NS, 30), "o_spool": (128, 2, NS, 15), "o_ssc": (128, 2, NS, 2),
        "o_swkv": (128, 2, NS, 64), "o_wkv": (128, 2, 64),
    }
    nc = bacc.Bacc("TRN2", target_bir_lowering=False, num_devices=1)
    feed, args = {}, {}
    for name, arr in arrays.items():
        arr = np.ascontiguousarray(arr)
        feed["in_" + name] = arr
        args[name] = nc.dram_tensor("in_" + name, arr.shape, mybir.dt.from_np(arr.dtype), kind="ExternalInput").ap()
    for name, shape in outs.items():
        args[name] = nc.dram_tensor("out_" + name, shape, F32, kind="ExternalOutput").ap()
    build(nc, args)
    r = run(nc, [feed], core_ids=[0]).results[0]
    o = {name: np.asarray(r["out_" + name]) for name in outs}

    def rows_of(v):
        v = v.swapaxes(0, 1)
        return np.ascontiguousarray(np.moveaxis(v.reshape((-1,) + v.shape[2:]), 0, -1))

    shift = rows_of(o["o_shift"])
    back = np.empty_like(shift)
    back[:, rw] = shift
    tails = o["o_tails"].reshape(128, 2, 47)
    wkv_p = o["o_wkv"].reshape(2, 64, 2, 64).transpose(2, 0, 3, 1).reshape(4, 64, 64)
    wkv_s = o["o_swkv"].reshape(2, 64, 2, NS, 64).transpose(3, 2, 0, 4, 1).reshape(NS, 4, 64, 64)
    return (
        o["yp"][None], o["ys"][:, None],
        rows_of(tails[:, :, 0:30])[None, None], rows_of(o["o_sconf"])[None],
        back[0][None, None], back[1:][None],
        wkv_p[None, None], wkv_s[None],
        rows_of(tails[:, :, 45:47])[None, None], rows_of(o["o_ssc"])[None],
        rows_of(tails[:, :, 30:45])[None, None], rows_of(o["o_spool"])[None],
    )
```

```python
from contextlib import ExitStack

import numpy as np

import concourse.bass as bass
from concourse import mybir

F32 = mybir.dt.float32
U32 = mybir.dt.uint32
ALU = mybir.AluOpType
ACT = mybir.ActivationFunctionType
AX = mybir.AxisListType

D = 1024
KT = D // 128
SEQ = 512
NS = 8
NT = SEQ + NS
TILES = SEQ // 128
GW = 256
CK = 31
SK = 3
PB = 15
NZ = 19
HEADS = 8
TOPK = 16
NEXP = 16384
CH = 64
NCH = SEQ // CH
UN = 2 * NCH
LEVELS = 6
HALF = NT // 2
DECAY = float(np.exp(-0.5))
NEG = -3.4e38

Z_GLU, Z_GATE, Z_LORA, Z_K, Z_R, Z_V, Z_B, Z_C, Z_H, Z_D = 0, 2, 4, 5, 7, 9, 11, 13, 15, 17


def column_order():
    a, b = 2 * GW, 2 * GW + 896
    r = range(a, a + 256)
    wlo = range(a + 256, a + 288)
    k = range(a + 288, a + 544)
    v = range(a + 544, a + 800)
    alo = range(a + 800, a + 832)
    glo = range(a + 832, a + 896)
    out = list(range(0, a))
    for part in (wlo, alo, glo, k, r, v):
        out += part
    return np.array(out + list(range(b, b + 1024)))


COLUMNS = {}
_n = 0
for _name, _w in [("g1", 8), ("mu", 7), ("w0", 2), ("a0", 2), ("kk", 2), ("ka", 2), ("rk", 2), ("lng", 2),
                  ("lnb", 2), ("cw", 2 * CK), ("cb", 2), ("clg", 2), ("clb", 2), ("sw", 2 * SK), ("ps", 2)]:
    COLUMNS[_name] = (_n, _w)
    _n += _w
NCOL = _n

CONSTS = {}
_n = 0
for _name, _w in [("ident", 128), ("blk", 128), ("blk64", 128), ("all256", 128), ("strict", 128), ("incl", CH),
                  ("levels", LEVELS * CH), ("scan", SEQ), ("invcnt", 32), ("iota", TOPK), ("sel", 64),
                  ("sel2", 8), ("hmask", 8), ("imask", 64)]:
    CONSTS[_name] = (_n, _w)
    _n += _w
NCONST = _n


def constants():
    p = np.arange(128)
    c = {}
    c["ident"] = np.eye(128)
    c["blk"] = (p[:, None] // 64 == p[None] // 64).astype(float)
    c["blk64"] = c["blk"] / 64
    c["all256"] = np.full((128, 128), 1 / 256)
    s, t = p % CH, np.arange(CH)
    c["strict"] = ((s[:, None, None] < t) & (p[:, None, None] // CH == np.arange(2)[None, :, None])).reshape(128, -1)
    c["incl"] = s[:, None] <= t[None]
    lv = np.zeros((128, LEVELS, CH))
    for i in range(LEVELS):
        b = 1 << i
        lv[:, i] = ((s[:, None] // (2 * b) == t[None] // (2 * b)) & (s[:, None] % (2 * b) < b)
                    & (t[None] % (2 * b) >= b))
    c["levels"] = lv.reshape(128, -1)
    c["scan"] = np.tile((np.arange(SEQ) % CH != 0).astype(float), (128, 1))
    cnt = np.zeros((128, 2, 16))
    for cc in range(2):
        for q in range(128):
            win = 2 << (2 * cc + q // 64)
            cnt[q, cc] = 1.0 / np.minimum(win, np.arange(16) + 1)
    c["invcnt"] = cnt.reshape(128, -1)
    c["iota"] = np.tile(np.arange(TOPK), (128, 1))
    c["sel"] = (p[:, None] == np.arange(64)[None] % 8).astype(float)
    c["sel2"] = (p[:, None] % 8 == np.arange(8)[None]).astype(float)
    c["hmask"] = (p[:, None] // 8 == np.arange(8)[None]).astype(float)
    c["imask"] = (p[:, None] % 64 == np.arange(64)[None]).astype(float)
    return np.concatenate([c[n].astype(np.float32) for n in CONSTS], 1)


RING = 8
ROW = 2 * D
LEAD = 2


def build(nc, a):
    ctx = ExitStack()
    with ctx:
        def sem(name):
            return ctx.enter_context(nc.semaphore(name))

        SIZE = 53200
        arena = ctx.enter_context(nc.sbuf_tensor("arena", [128, SIZE], F32))
        ps = ctx.enter_context(nc.psum_tensor("ps", [128, 8, 512], F32))
        top = [0]

        def at(off, *shape):
            n = int(np.prod(shape))
            assert off + n <= SIZE
            v = arena[:, off:off + n]
            names = "abcd"[:len(shape)]
            if len(shape) > 1:
                v = v.rearrange(f"p ({' '.join(names)}) -> p {' '.join(names)}",
                                **{names[i]: shape[i] for i in range(1, len(shape))})
            return v

        def take(*shape):
            off = top[0]
            top[0] += int(np.prod(shape))
            return off, at(off, *shape)

        _, x = take(TILES + 1, D)
        o_xn, xn = take(TILES + 1, D)
        o_h, hT = take(KT, NT)
        _, const = take(NCONST)
        _, cols = take(NCOL)
        _, rows = take(2, D)
        _, st = take(4, TILES + 1)
        _, eps = take(2)
        o_ext, extc = take(2, NS, CK)
        _, extp = take(2, NS, PB + 1)
        _, extq = take(2, NS, SK)
        _, wc = take(2, NCH)
        _, tails = take(2, 30 + 15 + 2)
        _, poolw = take(2, 128)
        _, carrier = take(2)
        carrier = carrier[0:1]
        o_z, z = take(NZ, NT)
        o_xs, xs = take(7, NT)
        o_w, wring = take(3, KT, 128)
        o_y, yT = take(8, NT)
        o_t, _ = take(12, 2 * NT)

        def cst(name):
            o, w = CONSTS[name]
            return const[:, o:o + w]

        def col(name, i=0, n=1):
            o, w = COLUMNS[name]
            return cols[:, o + i:o + i + n]

        ident, blk, blk64, all256, incl = (cst(n) for n in ("ident", "blk", "blk64", "all256", "incl"))
        strict = cst("strict").rearrange("p (a t) -> p a t", t=CH)
        levels = cst("levels").rearrange("p (l t) -> p l t", t=CH)
        imask = cst("imask")

        sgw, cum, ee, ei, ex, kk, kp, tmp, bb, aa, gg, bonus = (at(o_t + i * 2 * NT, 2, NT) for i in range(12))
        loraw = at(o_t + 11 * 2 * NT, GW)
        lt = at(o_t + 4 * 2 * NT, NT)
        UW = UN * 128
        ar = at(o_z, 2, NCH, 2, CH)
        a_bd, b_bd = at(o_xn, UN, 128), at(o_xn + UW, UN, 128)
        k_bd, v_bd = at(o_z + UW, UN, 128), at(o_t, UN, 128)
        lt_bd = at(o_t + 4 * NT, UN, 128)
        mt_bd = at(o_t + 4 * NT + UW, UN, 128)
        atok, btok = at(o_t + 4 * NT + 2 * UW, UN, 128), at(o_t + 4 * NT + 3 * UW, UN, 128)
        ktok, vtok = at(o_xs, UN, 128), at(o_w, UN, 128)
        grb, grk = at(o_xs + UW, UN, CH), at(o_xn + 2 * UW, UN, CH)
        tinv, tinvt, u_sb, lm = a_bd, b_bd, k_bd, v_bd
        mv, p1t, p2 = mt_bd, lt_bd, u_sb
        state = at(o_w + UW, 2, 2, 128)
        sa = at(o_w + UW + 512, 2, 2, 128)
        sst = at(o_z + 2 * UW, 2, NS, CH)
        smp = at(o_z + 2 * UW + 1024, 6, 2, NS)
        decayed = at(o_z + 2 * UW + 1024 + 96, 2, 128)
        tmp_ln = at(o_z + UW, 2, NT)
        assert 4 * NT + 4 * UW <= 20 * NT and 2 * UW + 1024 + 96 + 256 <= Z_B * NT
        gpad = at(o_xn, 2, CK - 1 + SEQ)
        cacc = at(o_xn + 1084, 2, NT)
        csq = at(o_xn + 2124, 2, NT)
        ctmp = at(o_xn + 3164, 2, NS, CK)
        W = PB + SEQ
        ppad, pa, pb = (at(o_h + i * 2 * W, 2, W) for i in range(3))
        ea, eb = (at(o_h + 6 * W + i * 256, 2, NS, PB + 1) for i in range(2))
        pw = yT[:, 6:8, :]
        qpad = at(o_h, 2, SK - 1 + SEQ)
        qtmp = at(o_h + 2 * (SK - 1 + SEQ), 2, SEQ)
        qs = at(o_h + 2 * (SK - 1 + SEQ) + 2 * SEQ, 2, NS)
        sp = at(o_h + 2112, 2, NS, CH)
        ssp = at(o_h + 2112 + 1024, 2, NS, CH)
        wout = at(o_t, KT, D)
        ring = at(o_z, RING, ROW)
        assert RING * ROW <= o_y - o_z
        junk = at(o_t, 2, D)
        xrep = at(o_t + 2 * D, D)
        cand = at(o_ext, TOPK, TOPK)
        candf = at(o_ext, 256)
        onehot = at(o_ext + 256, 2, TOPK, TOPK)
        scores = at(o_ext + 256, 256)
        e = o_t + KT * D
        wq = at(e, KT, 256)
        k12 = at(e + 2048, 2, 128)
        wqk = at(e, 2048 + 256)
        e += 2048 + 256
        diag = at(e, 4, 128)
        e += 512
        qT = at(e, 2, 128)
        e += 256
        qrep = at(e, 2, 64)
        e += 128
        sscore = at(e, 2, 128)
        e += 256
        v16 = at(e, 2, TOPK)
        e += 32
        i16 = at(e, 2 * TOPK).bitcast(U32).rearrange("p (a b) -> p a b", b=TOPK)
        e += 32
        i16f = at(e, 2, TOPK)
        e += 32
        scr = at(e, 256)
        e += 256
        sc16 = at(e, TOPK)
        e += 16
        pos = at(e, TOPK).bitcast(U32)
        e += 16
        abu = at(e, 2 * TOPK).bitcast(U32)
        e += 32
        abf = at(e, 2 * TOPK)
        e += 32
        ef = at(e, 2, TOPK)
        e += 32
        negm = at(e, 1)
        e += 1
        ssum = at(e, 2)
        e += 3
        idx = at(e, 5 * TOPK).bitcast(U32).rearrange("p (a b) -> p a b", b=TOPK)
        e += 80
        gate = at(e, 5, TOPK)
        e += 80
        hsel = at(e, 2, TOPK)
        e += 32
        gl = at(e, 2, TOPK)
        e += 32
        wgt = at(e, 2, TOPK)
        e += 32
        assert e <= o_t + 12 * 2 * NT

        d_const, d_cols, d_rows, d_small, d_out = (sem(n) for n in ("d_const", "d_cols", "d_rows", "d_small", "d_out"))
        d_x = [sem(f"d_x{t}") for t in range(TILES + 1)]
        d_w = [sem(f"d_w{i}") for i in range(3)]
        d_sst, d_wqk, d_wout, d_shift, d_swkv = (sem(n) for n in ("d_sst", "d_wqk", "d_wout", "d_shift", "d_swkv"))
        d_row = [sem(f"d_row{i}") for i in range(RING)]
        act_chain, dve_chain, pool_chain = sem("act_chain"), sem("dve_chain"), sem("pool_chain")
        names = """sq_done mean_done root_done xn_done turned hT_done z_done z_copied
            gate_done glu_done conf_sum conf_centered conf_sq conf_var conf_root conf_u conf_sig conf_out
            xs_done lora_act lora_mm lora_out kk_sq kk_sum kk_max kk_root bonus_in bonus_sum bonus_done
            cum_done exp_done zero_k zero_ab zero_v a_ready av_bd composites smp_ready
            pool_in pool_mm pool_out short_done tails_done sample_in sample_mm sample_copied samp_state samp_out
            turned_tok tok_copied g_mm g_masked lm_ready u_mm u_copied v_mm l1_mm
            mv_mm mv_copied p_mm p1_copied p2_copied sa_mm x_ready s_mm y_mm y_copied state_ready
            ln_sum ln_sq ln_root rwkv_out out_mm x1_done sq2 mean2 root2 xn2_done turned2 hT2_done
            xrep_mm xrep_done q_mm q_copied score_mm score_used exp_in exp2_done idx_ready
            dot_done gelu_done diag_done slot_used unit_mm unit_added sq_mm sq_copied ss_mm ss_added
            carried fin_sq fin_mean fin_root fin_done""".split()
        S = {n: sem(n) for n in names}
        weight_done = sem("weight_done")
        block = ctx.enter_context(nc.Block())

        def halves(v):
            return v.rearrange("p a (h c) -> p (a h) c", c=HALF)

        def banks(b, n=4):
            return ps[:, b:b + n, 0:HALF]

        def by_chunk(v, cc):
            return v[:, cc, 0:SEQ].rearrange("p (n t) -> p n t", t=CH)

        @block.sync
        def _(sp_):
            sp_.dma_start(const, a["const"][:, :]).then_inc(d_const, 16)
            sp_.dma_start(cols, a["cols"][:, :]).then_inc(d_cols, 16)
            for t in range(TILES):
                sp_.dma_start(x[:, t, :], a["xp"][128 * t:128 * t + 128, :]).then_inc(d_x[t], 16)
            sp_.dma_start(x[0:NS, TILES, :], a["xs"][:, :]).then_inc(d_x[TILES], 16)

            def weights(i):
                if i >= 3:
                    sp_.wait_ge(S["z_done"], i - 2)
                sp_.dma_start(wring[:, i % 3, :, :].rearrange("p a b -> p (a b)"), a["win"][i]).then_inc(d_w[i % 3], 16)

            for i in range(3):
                weights(i)
            sp_.dma_start(extc[:, :, :, 0:CK - 1], a["sconf"][:, :, :, :]).then_inc(d_small, 16)
            sp_.dma_start(extp[:, :, :, 0:PB], a["spool"][:, :, :, :]).then_inc(d_small, 16)
            sp_.dma_start(extq[:, :, :, 0:SK - 1], a["ssc"][:, :, :, :]).then_inc(d_small, 16)
            sp_.dma_start(loraw, a["lora"][:, :]).then_inc(d_small, 16)
            sp_.dma_start(poolw, a["poolw"][:, :, :]).then_inc(d_small, 16)
            sp_.dma_start(yT[:, 0:7, 512:520], a["sshift"][:, :, :]).then_inc(d_small, 16)
            for i in range(3, 8):
                weights(i)
            sp_.dma_start(rows[:, 0, :], a["n2"][0:1, :].partition_broadcast(128).rearrange("p a n -> p (a n)")).then_inc(d_rows, 16)
            sp_.dma_start(rows[:, 1, :], a["nf"][0:1, :].partition_broadcast(128).rearrange("p a n -> p (a n)")).then_inc(d_rows, 16)
            for i in range(8, Z_C):
                weights(i)
            sp_.wait_ge(S["z_copied"], Z_B)
            sp_.dma_start(a["o_shift"][:, :, :], z[:, Z_LORA:Z_B, SEQ - 1:NT]).then_inc(d_shift, 16)
            for i in range(Z_C, Z_H):
                weights(i)
            sp_.wait_ge(d_shift, 16)
            sp_.wait_ge(S["xs_done"], 7)
            sp_.dma_start(sst, a["swkv"][:, :, :, :]).then_inc(d_sst, 16)
            for i in range(Z_H, NZ):
                weights(i)
            sp_.wait_ge(S["conf_sum"], 1)
            sp_.dma_start(a["o_sconf"][:, :, :, :], extc[:, :, :, 1:CK]).then_inc(d_out, 16)
            sp_.wait_ge(S["tails_done"], 2)
            sp_.wait_ge(S["conf_sum"], 1)
            sp_.dma_start(a["o_tails"][:, :], tails.rearrange("p a b -> p (a b)")).then_inc(d_out, 16)
            sp_.dma_start(a["o_spool"][:, :, :, :], extp[:, :, :, 1:PB + 1]).then_inc(d_out, 16)
            sp_.dma_start(a["o_ssc"][:, :, :, :], extq[:, :, :, 1:SK]).then_inc(d_out, 16)
            sp_.wait_ge(S["samp_state"], 1)
            sp_.dma_start(a["o_swkv"][:, :, :, :], sst).then_inc(d_swkv, 16)
            sp_.wait_ge(S["y_mm"], NCH)
            for k in range(0, KT, 2):
                sp_.dma_start(wout[:, k:k + 2, :], a["wout"][:, k:k + 2, :]).then_inc(d_wout, 16)
            sp_.wait_ge(S["state_ready"], NCH + 1)
            for par in range(2):
                r = slice(64 * par, 64 * par + 64)
                sp_.dma_start(a["o_wkv"][r, :, :], state[r, NCH % 2, :, r]).then_inc(d_out, 16)

            sp_.wait_ge(S["rwkv_out"], 1)
            sp_.dma_start(wqk, a["wqk"][0]).then_inc(d_wqk, 16)
            with sp_.Fori(0, HEADS - 1) as h:
                sp_.wait_ge(S["score_mm"], TILES * (h + 1))
                sp_.wait_ge(S["ss_mm"], h + 1)
                sp_.dma_start(wqk, a["wqk"][bass.ds(h + 1, 1), :, :].rearrange("a p n -> (a p) n")).then_inc(d_wqk, 16)
            for t in range(TILES + 1):
                sp_.wait_ge(S["fin_done"], t + 1)
                if t < TILES:
                    sp_.dma_start(a["yp"][128 * t:128 * t + 128, :], xn[:, t, :]).then_inc(d_out, 16)
                else:
                    sp_.dma_start(a["ys"][:, :], xn[0:NS, TILES, :]).then_inc(d_out, 16)
            sp_.wait_ge(d_out, 16 * (6 + TILES + 1))

        @block.tensor
        def _(pe):
            mm, turn = nc.tensor.matmul, nc.tensor.transpose

            def turn_rows(t, b, ready, out):
                n = 128 if t < TILES else NS
                pe.wait_ge(S[ready], t + 1)
                for k in range(KT):
                    last = turn(ps[:, b + k // 4, (k % 4) * 128:(k % 4) * 128 + n],
                                xn[0:n, t, 128 * k:128 * k + 128], ident[0:n, 0:n])
                last.then_inc(S[out], 1)

            def sums(mat, src, b, joint=False):
                for h in range(2):
                    for cc in range(2):
                        last = mm(ps[:, b + (h if joint else 2 * cc + h), 0:HALF], mat, src[:, cc, HALF * h:HALF * h + HALF],
                                  start=(cc == 0 or not joint), stop=(cc == 1 or not joint))
                return last

            pe.wait_ge(d_const, 16)
            for t in range(TILES + 1):
                if t >= 2:
                    pe.wait_ge(S["hT_done"], t - 1)
                turn_rows(t, 4 + 2 * (t % 2), "xn_done", "turned")
            pe.wait_ge(S["hT_done"], TILES + 1)

            def project(i):
                pe.wait_ge(d_w[i % 3], 16 * (i // 3 + 1))
                if i >= 2:
                    pe.wait_ge(S["z_copied"], i - 1)
                for h in range(2):
                    for k in range(KT):
                        last = mm(ps[:, 2 * (i % 2) + h, 0:HALF], wring[:, i % 3, k, :], hT[:, k, HALF * h:HALF * h + HALF],
                                  start=(k == 0), stop=(k == KT - 1))
                last.then_inc(S["z_done"], 1)

            for i in range(Z_B):
                project(i)
            pe.wait_ge(S["conf_sum"], 1)
            sums(all256, cacc, 4, joint=True).then_inc(S["conf_centered"], 1)
            project(Z_B)
            pe.wait_ge(S["conf_sq"], 1)
            sums(all256, csq, 6, joint=True).then_inc(S["conf_var"], 1)
            pe.wait_ge(S["lora_act"], 1)
            pe.wait_ge(d_small, 16 * 6)
            pe.wait_ge(S["conf_root"], 1)
            for n, (lo, hi) in enumerate([(0, 32), (32, 64), (64, 128)]):
                if n:
                    project(Z_B + n)
                    pe.wait_ge(S["lora_out"], n)
                for cc in range(2):
                    for h in range(2):
                        last = mm(ps[:, 4 + 2 * cc + h, 0:HALF], loraw[lo:hi, 128 * cc:128 * cc + 128],
                                  lt[lo:hi, HALF * h:HALF * h + HALF], start=True, stop=True)
                last.then_inc(S["lora_mm"], 1)
            pe.wait_ge(S["kk_sq"], 1)
            pe.wait_ge(S["lora_out"], 3)
            sums(blk, tmp, 4).then_inc(S["kk_sum"], 1)
            project(Z_C + 1)
            project(Z_H)
            pe.wait_ge(S["bonus_in"], 1)
            sums(blk, tmp, 4).then_inc(S["bonus_sum"], 1)
            for i in range(Z_H + 1, NZ):
                project(i)

            pe.wait_ge(S["z_copied"], NZ)
            for g in range(4 * 4):
                src = (v_bd, a_bd, b_bd, k_bd)[g // 4]
                q = g % 4
                if g < 8:
                    pe.wait_ge(S["av_bd"], q // 2 + 1)
                elif g == 8:
                    pe.wait_ge(S["composites"], 1)
                if g >= 4:
                    pe.wait_ge(S["tok_copied"], g - 3)
                for j in range(4):
                    last = turn(ps[:, q, 128 * j:128 * j + 128], src[:, 4 * q + j, :], ident)
                last.then_inc(S["turned_tok"], 1)
            pe.wait_ge(S["bonus_done"], 1)
            for q in range(4):
                if q >= 2:
                    pe.wait_ge(S["g_masked"], q - 1)
                for i, src in enumerate((b_bd, k_bd)):
                    for j in range(4):
                        u = 4 * q + j
                        last = mm(ps[:, 4 + 2 * (q % 2) + i, 128 * j:128 * j + 128], src[:, u, :],
                                  ar[:, u // NCH, u % NCH].rearrange("p a b -> p (a b)"), start=True, stop=True)
                last.then_inc(S["g_mm"], 1)

            def four(q, bank, left, right):
                for j in range(4):
                    last = mm(ps[:, bank, 128 * j:128 * j + 128], left[:, 4 * q + j, :],
                              right if right is ident else right[:, 4 * q + j, :], start=True, stop=True)
                return last

            pe.wait_ge(S["tok_copied"], 16)
            for q in range(4):
                pe.wait_ge(S["lm_ready"], q + 1)
                four(q, q, lm, ident).then_inc(S["l1_mm"], 1)

            def sample_sum(n):
                pe.wait_ge(S["sample_in"], n + 1)
                b = 2 * (n % 2)
                for cc in range(2):
                    last = mm(ps[:, b + cc, :], blk, sp[:, cc, :, :].rearrange("p a b -> p (a b)"), start=True, stop=True)
                last.then_inc(S["sample_mm"], 1)

            pe.wait_ge(S["g_masked"], 4)
            for lv in range(1, LEVELS):
                for first in (0, 2):
                    for q in (first, first + 1):
                        n = 4 * (lv - 1) + q
                        pe.wait_ge(S["lm_ready"], n + 7 if n >= 2 else n + 5)
                        four(q, 4 + 2 * (q % 2), lm, tinv).then_inc(S["u_mm"], 1)
                    for q in (first, first + 1):
                        pe.wait_ge(S["u_copied"], 4 * (lv - 1) + q + 1)
                        if lv < LEVELS - 1:
                            four(q, 5 + 2 * (q % 2), tinvt, u_sb)
                        four(q, 4 + 2 * (q % 2), u_sb, tinvt).then_inc(S["v_mm"], 1)
                if lv == 2:
                    pe.wait_ge(S["pool_in"], 1)
                    for cc in range(2):
                        for h in range(2):
                            last = mm(ps[:, 2 * cc + h, 0:HALF], poolw[:, cc, :], pw[:, cc, HALF * h:HALF * h + HALF],
                                      start=True, stop=True)
                    last.then_inc(S["pool_mm"], 1)
                if lv == 3:
                    pe.wait_ge(S["pool_out"], 1)
                    sample_sum(0)
                if lv == 4:
                    sample_sum(1)
            pe.wait_ge(S["lm_ready"], 4 * LEVELS + 4)
            for first in (0, 2):
                for q in (first, first + 1):
                    if q >= 2:
                        pe.wait_ge(S["p1_copied"], q - 1)
                        pe.wait_ge(S["p2_copied"], q - 1)
                    four(q, 4 + 2 * (q % 2), mt_bd, vtok).then_inc(S["mv_mm"], 1)
                for q in (first, first + 1):
                    four(q, 5 + 2 * (q % 2), atok, tinvt)
                    pe.wait_ge(S["mv_copied"], q + 1)
                    four(q, 4 + 2 * (q % 2), tinvt, mv).then_inc(S["p_mm"], 1)
            sample_sum(2)
            pe.wait_ge(S["p1_copied"], 4)
            pe.wait_ge(S["p2_copied"], 4)
            pe.wait_ge(S["samp_out"], 1)
            for c in range(NCH):
                now = state[:, c % 2]
                yb_ = 6 if c % 2 == 0 else 2
                pe.wait_ge(S["state_ready"], c + 1)
                for cc in range(2):
                    last = mm(ps[:, 0, 128 * cc:128 * cc + 128], p1t[:, NCH * cc + c, :], now[:, cc, :], start=True, stop=True)
                last.then_inc(S["sa_mm"], 1)
                if c >= 2:
                    pe.wait_ge(S["y_copied"], c - 1)
                for cc in range(2):
                    u = NCH * cc + c
                    mm(ps[:, 4 + cc, 0:128], ktok[:, u, :], vtok[:, u, :], start=True, stop=False)
                    mm(ps[:, yb_ + cc, 0:CH], now[:, cc, :], ar[:, cc, c, 1, :], start=True, stop=False)
                    mm(ps[:, yb_ + cc, 0:CH], vtok[:, u, :], grk[:, u, :], start=False, stop=False)
                pe.wait_ge(S["x_ready"], c + 1)
                for cc in range(2):
                    last = mm(ps[:, 4 + cc, 0:128], btok[:, NCH * cc + c, :], sa[:, c % 2, cc, :], start=False, stop=True)
                last.then_inc(S["s_mm"], 1)
                for cc in range(2):
                    last = mm(ps[:, yb_ + cc, 0:CH], sa[:, c % 2, cc, :], grb[:, NCH * cc + c, :], start=False, stop=True)
                last.then_inc(S["y_mm"], 1)
            pe.wait_ge(S["y_copied"], NCH)
            pe.wait_ge(S["state_ready"], NCH + 1)
            sums(blk64, yT[:, 2:4, :], 4).then_inc(S["ln_sum"], 1)
            pe.wait_ge(S["ln_sq"], 1)
            sums(blk64, tmp_ln, 0).then_inc(S["ln_sum"], 1)

            def project_out(t):
                n = 128 if t < TILES else NS
                if t >= 2:
                    pe.wait_ge(S["x1_done"], t - 1)
                for nh in range(2):
                    for k in range(KT):
                        last = mm(ps[0:n, 2 * (t % 2) + nh, :], yT[:, k, 128 * t:128 * t + n],
                                  wout[:, k, 512 * nh:512 * nh + 512], start=(k == 0), stop=(k == KT - 1))
                last.then_inc(S["out_mm"], 1)

            def turn_normed(t):
                if t:
                    pe.wait_ge(S["hT2_done"], t)
                turn_rows(t, 6, "xn2_done", "turned2")

            def query(h, t):
                v = TILES * h + t
                if t == 0:
                    pe.wait_ge(d_wqk, 16 * (h + 1))
                if not (isinstance(h, int) and v == 0):
                    pe.wait_ge(S["q_copied"], v)
                for half in range(2):
                    for k in range(KT):
                        last = mm(ps[:, 4, 128 * half:128 * half + 128], wq[:, k, 128 * half:128 * half + 128],
                                  hT[:, k, 128 * t:128 * t + 128], start=(k == 0), stop=(k == KT - 1))
                last.then_inc(S["q_mm"], 1)

            def score(h, t):
                v = TILES * h + t
                pe.wait_ge(S["q_copied"], v + 1)
                if not (isinstance(h, int) and v == 0):
                    pe.wait_ge(S["score_used"], v)
                for half in range(2):
                    last = mm(ps[:, 5, 128 * half:128 * half + 128], qT[:, half, :], k12[:, half, :], start=True, stop=True)
                last.then_inc(S["score_mm"], 1)

            def sample_query(h):
                if not (isinstance(h, int) and h == 0):
                    pe.wait_ge(S["ss_added"], h)
                for half in range(2):
                    for k in range(KT):
                        last = mm(ps[:, 6, 256 + 8 * half:264 + 8 * half], wq[:, k, 128 * half:128 * half + 128],
                                  hT[:, k, SEQ:NT], start=(k == 0), stop=(k == KT - 1))
                last.then_inc(S["sq_mm"], 1)
                pe.wait_ge(S["sq_copied"], h + 1)
                for half in range(2):
                    last = mm(ps[0:64, 6, 128 * half:128 * half + 128], qrep[:, half, :], k12[:, half, :], start=True, stop=True)
                last.then_inc(S["ss_mm"], 1)

            def prepare(h, t, step):
                if step == 0:
                    query(h, t)
                else:
                    score(h, t)
                    if t == 0:
                        sample_query(h)

            def unit(h, t, nxt):
                u = TILES * h + t
                n = 128 if t < TILES else 64
                m = 128 if t < TILES else NS
                b = 2 * (t % 2)
                pe.wait_ge(S["unit_added"], u + 1)
                for s in range(TOPK):
                    pe.wait_ge(S["diag_done"], TOPK * u + s + 1)
                    for c in range(2):
                        last = mm(ps[0:m, b + c, :], diag[0:n, s % 4, 0:m], ring[0:n, s % RING, D + 512 * c:D + 512 * c + 512],
                                  start=(s == 0), stop=(s == TOPK - 1))
                    last.then_inc(S["slot_used"], 1)
                    if nxt and s in (3, 5):
                        prepare(nxt[0], nxt[1], 0 if s == 3 else 1)

            pe.sem_inc(S["slot_used"], RING)
            pe.sem_inc(S["unit_added"], 2)
            for n in ("conf_out", "rwkv_out", "short_done", "pool_out"):
                pe.wait_ge(S[n], 1)
            pe.wait_ge(d_wout, 16 * (KT // 2))
            for t in range(TILES + 1):
                project_out(t)
                turn_normed(t)
                if t < LEAD:
                    pe.wait_ge(S["hT2_done"], t + 1)
                    query(0, t)
                    score(0, t)
            pe.wait_ge(S["hT2_done"], TILES + 1)
            for n in range(2):
                last = mm(ps[0:64, n, :], cst("sel")[0:NS, :], xn[0:NS, TILES, 512 * n:512 * n + 512], start=True, stop=True)
            last.then_inc(S["xrep_mm"], 1)
            pe.wait_ge(S["xrep_done"], 1)
            sample_query(0)
            with pe.Fori(0, HEADS - 1) as h:
                for t in range(TILES):
                    unit(h, t, (h, t + LEAD) if t + LEAD < TILES else (h + 1, t + LEAD - TILES))
            for t in range(TILES):
                unit(HEADS - 1, t, (HEADS - 1, t + LEAD) if t + LEAD < TILES else None)
            unit(HEADS - 1, TILES, None)

        @block.scalar
        def _(act):
            f = nc.scalar.activation
            count = {}

            def link(ins, name=None):
                s = S[name] if name else act_chain
                count[name] = count.get(name, 0) + 1
                ins.then_inc(s, 1)
                act.wait_ge(s, count[name])

            def squares(t, ready, name, dst):
                n = 128 if t < TILES else NS
                f(dst[0:n, t, :], x[0:n, t, :], ACT.Square, accum_out=st[0:n, 0, t:t + 1]).then_inc(S[name], 1)

            def root(t, mean, name):
                n = 128 if t < TILES else NS
                act.wait_ge(S[mean], t + 1)
                f(st[0:n, 2, t:t + 1], st[0:n, 1, t:t + 1], ACT.Sqrt).then_inc(S[name], 1)

            act.wait_ge(d_const, 16)
            act.wait_ge(d_cols, 16)
            for t in range(TILES + 1):
                act.wait_ge(d_x[t], 16)
                squares(t, None, "sq_done", xn)
            for t in range(TILES + 1):
                root(t, "mean_done", "root_done")

            def copy_z(i):
                act.wait_ge(S["z_done"], i + 1)
                f(z[:, i, :].rearrange("p (h c) -> p h c", c=HALF), banks(2 * (i % 2), 2), ACT.Copy).then_inc(S["z_copied"], 1)

            for i in range(Z_LORA):
                copy_z(i)
            act.wait_ge(S["z_copied"], Z_LORA)
            f(z[:, Z_GATE:Z_GATE + 2, :], z[:, Z_GATE:Z_GATE + 2, :], ACT.Sigmoid).then_inc(S["gate_done"], 1)
            for i in range(Z_LORA, Z_B + 1):
                copy_z(i)
            act.wait_ge(S["xs_done"], 1)
            f(lt[0:32, :], xs[0:32, 0, :], ACT.Tanh)
            f(lt[32:64, :], xs[32:64, 0, :], ACT.Copy)
            f(lt[64:128, :], xs[64:128, 0, :], ACT.Sigmoid).then_inc(S["lora_act"], 1)
            act.wait_ge(S["conf_var"], 1)
            f(csq[:, 0, :].rearrange("p (h c) -> p h c", c=HALF), banks(6, 2), ACT.Sqrt, bias=eps[:, 0:1]).then_inc(S["conf_root"], 1)

            def lora(n, dst, fun, bias):
                act.wait_ge(S["lora_mm"], n + 1)
                for cc in range(2):
                    kw = {"bias": col(bias, cc)} if bias else {}
                    last = f(dst[:, cc, :].rearrange("p (h c) -> p h c", c=HALF), banks(4 + 2 * cc, 2), fun, **kw)
                last.then_inc(S["lora_out"], 1)

            lora(0, sgw, ACT.Sigmoid, "w0")
            copy_z(Z_B + 1)
            lora(1, aa, ACT.Sigmoid, "a0")
            copy_z(Z_C)
            lora(2, gg, ACT.Copy, None)
            act.wait_ge(S["conf_u"], 1)
            f(csq, cacc, ACT.Sigmoid).then_inc(S["conf_sig"], 1)
            act.wait_ge(S["kk_max"], 1)
            f(tmp, tmp, ACT.Sqrt).then_inc(S["kk_root"], 1)
            copy_z(Z_C + 1)
            act.wait_ge(S["cum_done"], 1)
            f(ee[:, :, 0:SEQ], cum[:, :, 0:SEQ], ACT.Exp, scale=-DECAY)
            f(ei[:, :, 0:SEQ], cum[:, :, 0:SEQ], ACT.Exp, scale=DECAY)
            act.wait_ge(S["xs_done"], 7)
            act.wait_ge(d_shift, 16)
            f(smp[:, 5], sgw[:, :, SEQ:NT], ACT.Exp, scale=-DECAY)
            f(ex[:, :, 0:SEQ], ex[:, :, 0:SEQ], ACT.Exp, scale=-DECAY).then_inc(S["exp_done"], 1)
            for i in range(Z_H, NZ - 1):
                copy_z(i)
            act.wait_ge(S["zero_v"], 1)
            act.wait_ge(S["zero_ab"], 1)
            for cc in range(2):
                for par in range(2):
                    r = slice(64 * par, 64 * par + 64)
                    f(v_bd[r, NCH * cc:NCH * cc + NCH, r], by_chunk(xs[:, 5:7], cc)[r], ACT.Copy)
                act.wait_ge(S["a_ready"], cc + 1)
                for par in range(2):
                    r = slice(64 * par, 64 * par + 64)
                    last = f(a_bd[r, NCH * cc:NCH * cc + NCH, r], ar[r, cc, :, 0, :], ACT.Copy)
                last.then_inc(S["av_bd"], 1)
            copy_z(NZ - 1)

            for g in range(16):
                act.wait_ge(S["turned_tok"], g + 1)
                if g == 4:
                    act.wait_ge(S["composites"], 1)
                q = g % 4
                dst = (vtok, atok, btok, ktok)[g // 4]
                f(dst[:, 4 * q:4 * q + 4, :].rearrange("p a b -> p (a b)"), ps[:, q, :], ACT.Copy).then_inc(S["tok_copied"], 1)

            def quarter(dst, q, bank, name):
                f(dst[:, 4 * q:4 * q + 4, :].rearrange("p a b -> p (a b)"), ps[:, bank, :], ACT.Copy).then_inc(S[name], 1)

            def sample_copy(n):
                b = 2 * (n % 2)
                act.wait_ge(S["sample_mm"], n + 1)
                if n:
                    act.wait_ge(S["sample_in"], n + 1)
                f(ssp.rearrange("p a b c -> p a (b c)"), ps[:, b:b + 2, :], ACT.Copy).then_inc(S["sample_copied"], 1)

            for lv in range(1, LEVELS):
                for q in range(4):
                    act.wait_ge(S["u_mm"], 4 * (lv - 1) + q + 1)
                    quarter(u_sb, q, 4 + 2 * (q % 2), "u_copied")
                if lv == 2:
                    act.wait_ge(S["pool_mm"], 1)
                    for cc in range(2):
                        last = f(yT[:, 6 + cc, :].rearrange("p (h c) -> p h c", c=HALF), banks(2 * cc, 2), ACT.Copy, scale=col("ps", cc))
                    last.then_inc(S["pool_out"], 1)
                if lv in (3, 4):
                    sample_copy(lv - 3)
            for first in (0, 2):
                for q in (first, first + 1):
                    act.wait_ge(S["mv_mm"], q + 1)
                    quarter(mv, q, 4 + 2 * (q % 2), "mv_copied")
                for q in (first, first + 1):
                    act.wait_ge(S["p_mm"], q + 1)
                    quarter(p1t, q, 5 + 2 * (q % 2), "p1_copied")
            for c in range(NCH):
                act.wait_ge(S["y_mm"], c + 1)
                b = 6 if c % 2 == 0 else 2
                f(yT[:, 2:4, CH * c:CH * c + CH], ps[:, b:b + 2, 0:CH], ACT.Copy).then_inc(S["y_copied"], 1)
            act.wait_ge(S["ln_sum"], 2)
            f(halves(tmp_ln), banks(0), ACT.Sqrt, bias=eps[:, 1:2]).then_inc(S["ln_root"], 1)

            def root_of_squares(t):
                act.wait_ge(S["x1_done"], t + 1)
                squares(t, None, "sq2", xn)
                root(t, "mean2", "root2")

            def queries(h, t):
                v = TILES * h + t
                act.wait_ge(S["q_mm"], v + 1)
                if not (isinstance(h, int) and v == 0):
                    act.wait_ge(S["score_mm"], v)
                f(qT.rearrange("p a b -> p (a b)"), ps[:, 4, 0:256], ACT.Copy).then_inc(S["q_copied"], 1)

            def sample_queries(h):
                act.wait_ge(S["sq_mm"], h + 1)
                for half in range(2):
                    last = f(qrep[:, half, :].rearrange("p (a b) -> p a b", b=NS),
                             ps[:, 6, 256 + 8 * half:264 + 8 * half].unsqueeze(1).to_broadcast([128, 8, NS]), ACT.Copy)
                last.then_inc(S["sq_copied"], 1)

            def softmax(v, t):
                n = 128 if t < TILES else 64
                act.wait_ge(S["exp_in"], v + 1)
                f(gate[0:n, t, :], sc16[0:n, :], ACT.Exp, bias=negm[0:n, :], accum_out=ssum[0:n, 0:1]).then_inc(S["exp2_done"], 1)

            def unit(h, t, nxt):
                u = TILES * h + t
                n = 128 if t < TILES else 64
                b = t % 2
                for s in range(0, TOPK, 2):
                    act.wait_ge(S["dot_done"], TOPK * u + s + 2 + 2)
                    f(gl[0:n, b, s:s + 2], hsel[0:n, b, s:s + 2], ACT.Gelu).then_inc(S["gelu_done"], 1)
                    act.wait_ge(S["gelu_done"], (TOPK // 2) * u + s // 2 + 1)
                    for j in range(2):
                        last = f(wgt[0:n, b, s + j:s + j + 1], gl[0:n, b, s + j:s + j + 1], ACT.Copy,
                                 scale=gate[0:n, t, s + j:s + j + 1])
                    last.then_inc(weight_done, 1)
                    act.wait_ge(weight_done, (TOPK // 2) * u + s // 2 + 1)
                    for j in range(2):
                        act.wait_ge(S["slot_used"], TOPK * u + s + j - 3 + RING)
                        src = ident[0:n, :] if t < TILES else cst("sel2")[0:n, :]
                        f(diag[0:n, (s + j) % 4, 0:128 if t < TILES else NS], src, ACT.Copy,
                          scale=wgt[0:n, b, s + j:s + j + 1]).then_inc(S["diag_done"], 1)
                    if nxt and s == 2:
                        if nxt[1] < TILES:
                            queries(nxt[0], nxt[1])
                    if nxt and s == 6 and nxt[1] == 0:
                        sample_queries(nxt[0])
                    if nxt and s == TOPK - 4:
                        softmax(TILES * nxt[0] + nxt[1], nxt[1])

            for t in range(TILES + 1):
                root_of_squares(t)
                if t < LEAD:
                    queries(0, t)
                    softmax(t, t)
            act.wait_ge(S["xrep_mm"], 1)
            for n in range(2):
                last = f(xrep[0:64, 512 * n:512 * n + 512], ps[0:64, n, :], ACT.Copy)
            last.then_inc(S["xrep_done"], 1)
            sample_queries(0)
            with act.Fori(0, HEADS - 1) as h:
                for t in range(TILES):
                    unit(h, t, (h, t + LEAD) if t + LEAD < TILES else (h + 1, t + LEAD - TILES))

            def final(t):
                n = 128 if t < TILES else NS
                act.wait_ge(S["unit_added"], TILES * (HEADS - 1) + t + 1 + 2)
                f(xn[0:n, t, :], x[0:n, t, :], ACT.Square,
                  accum_out=st[0:n, 0, t:t + 1]).then_inc(S["fin_sq"], 1)
                act.wait_ge(S["fin_mean"], t + 1)
                f(st[0:n, 2, t:t + 1], st[0:n, 1, t:t + 1], ACT.Sqrt).then_inc(S["fin_root"], 1)

            last_h = HEADS - 1
            for t in range(TILES):
                nxt = (last_h, t + LEAD) if t + LEAD <= TILES else None
                unit(last_h, t, nxt)
            unit(last_h, TILES, None)
            for t in range(TILES + 1):
                final(t)

        @block.vector
        def _(dve):
            v = nc.vector
            count = {}

            def link(ins, name=None):
                s = S[name] if name else dve_chain
                count[name] = count.get(name, 0) + 1
                ins.then_inc(s, 1)
                dve.wait_ge(s, count[name])

            def tt(out, i0, i1, op):
                return v.tensor_tensor(out, i0, i1, op)

            def ts(out, i0, s1, op0, s2=None, op1=None):
                return v.tensor_scalar(out, i0, s1, s2, op0, op1) if op1 is not None else v.tensor_scalar(out, i0, s1, None, op0)

            def stt(out, i0, s, i1, op0, op1):
                return v.scalar_tensor_tensor(out=out, in0=i0, scalar=s, in1=i1, op0=op0, op1=op1)

            MUL, ADD, SUB, MAX = ALU.mult, ALU.add, ALU.subtract, ALU.max

            def features(t, turned, done, gain):
                n = 128 if t < TILES else NS
                dve.wait_ge(S[turned], t + 1)
                src = ps[:, 4 + 2 * (t % 2):6 + 2 * (t % 2), :].rearrange("p a (b c) -> p (a b) c", c=128)[:, :, 0:n]
                dst = hT[:, :, 128 * t:128 * t + n]
                if gain:
                    link(tt(dst, src, col("g1", 0, KT).unsqueeze(2).to_broadcast([128, KT, n]), MUL), done)
                else:
                    link(v.tensor_copy(dst, src), done)

            def mean(t, sq, name):
                n = 128 if t < TILES else NS
                dve.wait_ge(S[sq], t + 1)
                link(ts(st[0:n, 1, t:t + 1], st[0:n, 0, t:t + 1], 1.0 / D, MUL, 1e-6, ADD), name)

            v.memset(eps[:, 0:1], 1e-5)
            link(v.memset(eps[:, 1:2], 64e-5))
            dve.wait_ge(d_cols, 16)
            dve.wait_ge(d_const, 16)
            for t in range(TILES + 1):
                mean(t, "sq_done", "mean_done")
            for t in range(TILES + 1):
                n = 128 if t < TILES else NS
                dve.wait_ge(S["root_done"], t + 1)
                link(v.reciprocal(st[0:n, 3, t:t + 1], st[0:n, 2, t:t + 1]))
                link(ts(xn[0:n, t, :], x[0:n, t, :], st[0:n, 3, t:t + 1], MUL), "xn_done")
                if t >= 1:
                    features(t - 1, "turned", "hT_done", True)
            features(TILES, "turned", "hT_done", True)

            dve.wait_ge(d_small, 16 * 6)
            link(v.memset(gpad[:, :, 0:CK - 1], 0.0))
            dve.wait_ge(S["gate_done"], 1)
            link(tt(gpad[:, :, CK - 1:], z[:, 0:2, 0:SEQ], z[:, 2:4, 0:SEQ], MUL))
            link(tt(extc[:, :, :, CK - 1], z[:, 0:2, SEQ:NT], z[:, 2:4, SEQ:NT], MUL))
            link(v.tensor_copy(tails[:, :, 0:30], gpad[:, :, SEQ:SEQ + 30]))
            cw = col("cw", 0, 2 * CK).rearrange("p (a b) -> p a b", b=CK)
            for k in range(CK):
                for cc in range(2):
                    o, i = cacc[:, cc, 0:SEQ], gpad[:, cc, k:k + SEQ]
                    w = cw[:, cc, k:k + 1]
                    ins = ts(o, i, w, MUL, col("cb", cc), ADD) if k == 0 else stt(o, i, w, o, MUL, ADD)
                    if cc == 0:
                        ins.then_inc(dve_chain, 1)
                        count[None] += 1
                    else:
                        link(ins)
            for cc in range(2):
                link(tt(ctmp[:, cc], extc[:, cc], cw[:, cc:cc + 1, :].to_broadcast([128, NS, CK]), MUL))
                link(v.tensor_reduce(cacc[:, cc, SEQ:NT], ctmp[:, cc], AX.X, ADD))
                link(ts(cacc[:, cc, SEQ:NT], cacc[:, cc, SEQ:NT], col("cb", cc), ADD), "conf_sum" if cc else None)
            dve.wait_ge(S["z_copied"], Z_B)
            zr = z[:, Z_LORA:Z_B, :]
            link(tt(xs[:, :, 1:SEQ], zr[:, :, 0:SEQ - 1], zr[:, :, 1:SEQ], SUB))
            link(ts(xs[:, :, 0:1], zr[:, :, 0:1], -1.0, MUL))
            link(tt(xs[:, :, SEQ:NT], yT[:, 0:7, SEQ:NT], zr[:, :, SEQ:NT], SUB))
            for j in range(7):
                link(stt(xs[:, j, :], xs[:, j, :], col("mu", j), zr[:, j, :], MUL, ADD), "xs_done")
            dve.wait_ge(S["conf_centered"], 1)
            for cc in range(2):
                c2 = cacc[:, cc, :].rearrange("p (h c) -> p h c", c=HALF)
                link(tt(c2, c2, banks(4, 2), SUB))
            link(tt(csq, cacc, cacc, MUL), "conf_sq")
            dve.wait_ge(S["conf_root"], 1)
            link(v.reciprocal(csq[:, 0, :], csq[:, 0, :]))
            for cc in range(2):
                link(stt(cacc[:, cc, :], cacc[:, cc, :], col("clg", cc), csq[:, 0, :], MUL, MUL))
                link(ts(cacc[:, cc, :], cacc[:, cc, :], col("clb", cc), ADD), "conf_u" if cc else None)

            k_, r_, v_ = xs[:, 1:3], xs[:, 3:5], xs[:, 5:7]
            for cc in range(2):
                link(ts(kk[:, cc, :], k_[:, cc, :], col("kk", cc), MUL))
            link(tt(tmp, kk, kk, MUL), "kk_sq")
            dve.wait_ge(S["lora_out"], 1)
            for cc in range(2):
                link(v.tensor_tensor_scan(cum[:, cc, 0:SEQ], cst("scan"), sgw[:, cc, 0:SEQ], 0.0, MUL, ADD))
            dve.wait_ge(S["lora_out"], 2)
            for cc in range(2):
                link(ts(kp[:, cc, :], aa[:, cc, :], -1.0, ADD, col("ka", cc), MUL))
                link(stt(kp[:, cc, :], kp[:, cc, :], 1.0, k_[:, cc, :], ADD, MUL))
            dve.wait_ge(S["lora_mm"], 3)
            link(tt(ex[:, :, 0:SEQ], cum[:, :, 0:SEQ], sgw[:, :, 0:SEQ], SUB), "cum_done")
            dve.wait_ge(S["kk_sum"], 1)
            link(ts(halves(tmp), banks(4), 1e-24, MAX), "kk_max")
            dve.wait_ge(S["conf_sig"], 1)
            link(tt(yT[:, 0:2, :], cacc, csq, MUL), "conf_out")
            dve.wait_ge(S["kk_root"], 1)
            link(v.reciprocal(tmp, tmp))
            link(stt(kk, kk, -1.0, tmp, MUL, MUL))
            link(stt(bb, kk, -1.0, aa, MUL, MUL))
            for cc in range(2):
                link(stt(tmp[:, cc, :], r_[:, cc, :], col("rk", cc), kp[:, cc, :], MUL, MUL), "bonus_in" if cc else None)

            dve.wait_ge(d_shift, 16)
            for i, src in enumerate((kk, bb, kp, r_, v_)):
                link(v.tensor_copy(smp[:, i], src[:, :, SEQ:NT]), "smp_ready" if i == 4 else None)
            dve.wait_ge(S["exp_done"], 1)
            dve.wait_ge(S["zero_ab"], 1)
            dve.wait_ge(S["zero_k"], 1)
            for cc in range(2):
                link(tt(ar[:, cc, :, 0, :], by_chunk(kk, cc), by_chunk(ex, cc), MUL), "a_ready")
                for par in range(2):
                    r, u = slice(64 * par, 64 * par + 64), slice(NCH * cc, NCH * cc + NCH)
                    link(tt(b_bd[r, u, r], by_chunk(bb, cc)[r], by_chunk(ei, cc)[r], MUL))
                    link(tt(k_bd[r, u, r], by_chunk(kp, cc)[r], by_chunk(ei, cc)[r], MUL))
                link(tt(ar[:, cc, :, 1, :], by_chunk(r_, cc), by_chunk(ee, cc), MUL))
                link(v.tensor_copy(wc[:, cc, :], by_chunk(ee, cc)[:, :, CH - 1]))
            dve.wait_ge(S["bonus_sum"], 1)
            dve.wait_ge(S["av_bd"], 2)
            link(tt(halves(bonus), banks(4), halves(v_), MUL), "composites")
            for cc in range(2):
                link(ts(bonus[:, cc, :], bonus[:, cc, :], col("lnb", cc), ADD), "bonus_done" if cc else None)

            def as_heads(v_):
                return v_.rearrange("p u (a t) -> p (u a) t", t=CH)

            def lt_level(q, lv, name):
                s = slice(4 * q, 4 * q + 4)
                m = levels[:, lv:lv + 1, :].to_broadcast([128, 8, CH])
                link(tt(as_heads(lm[:, s, :]), as_heads(lt_bd[:, s, :]), m, MUL), name)

            eye = ident.unsqueeze(1).to_broadcast([128, 4, 128])

            def bank4(b):
                return ps[:, b, :].rearrange("p (a c) -> p a c", c=128)

            for q in range(4):
                s = slice(4 * q, 4 * q + 4)
                gb, gk = bank4(4 + 2 * (q % 2)), bank4(5 + 2 * (q % 2))
                smask = strict.unsqueeze(1).to_broadcast([128, 4, 2, CH])
                imask4 = incl.unsqueeze(1).to_broadcast([128, 4, CH])

                def spread_heads(v_):
                    return v_[:, :, 0:CH].unsqueeze(2).to_broadcast([128, 4, 2, CH])

                dve.wait_ge(S["g_mm"], q + 1)
                link(tt(lt_bd[:, s, :].rearrange("p u (a t) -> p u a t", t=CH), spread_heads(gb), smask, MUL))
                lt_level(q, 0, "lm_ready")
                link(tt(mt_bd[:, s, :].rearrange("p u (a t) -> p u a t", t=CH), spread_heads(gk), smask, MUL))
                link(tt(grb[:, s, :], gb[:, :, CH:128], imask4, MUL))
                if q == 0:
                    dve.wait_ge(S["tok_copied"], 16)
                link(tt(grk[:, s, :], gk[:, :, CH:128], imask4, MUL), "g_masked")
                link(tt(tinvt[:, s, :], lm[:, s, :], eye, ADD))
            for q in range(4):
                s = slice(4 * q, 4 * q + 4)
                dve.wait_ge(S["l1_mm"], q + 1)
                link(tt(tinv[:, s, :], bank4(q), eye, ADD))
                lt_level(q, 1, "lm_ready")
            for lv in range(1, LEVELS):
                for q in range(4):
                    s = slice(4 * q, 4 * q + 4)
                    dve.wait_ge(S["v_mm"], 4 * (lv - 1) + q + 1)
                    last = lv == LEVELS - 1
                    if not last:
                        link(tt(tinv[:, s, :], tinv[:, s, :], bank4(5 + 2 * (q % 2)), ADD))
                    link(tt(tinvt[:, s, :], tinvt[:, s, :], bank4(4 + 2 * (q % 2)), ADD), "lm_ready" if last else None)
                    if not last:
                        lt_level(q, lv + 1, "lm_ready")
            for q in range(4):
                dve.wait_ge(S["p_mm"], q + 1)
                link(v.tensor_copy(p2[:, 4 * q:4 * q + 4, :], bank4(4 + 2 * (q % 2))), "p2_copied")
            dve.wait_ge(S["sample_mm"], 3)
            for cc in range(2):
                link(tt(sp[:, cc], ps[:, cc, :].rearrange("p (b c) -> p b c", c=CH),
                        imask.unsqueeze(1).to_broadcast([128, NS, CH]), MUL))
                link(v.tensor_reduce(yT[:, 2 + cc, SEQ:NT], sp[:, cc], AX.X, ADD), "samp_out" if cc else None)
            for c in range(NCH):
                if c == 0:
                    dve.wait_ge(S["state_ready"], 1)
                link(tt(decayed, state[:, c % 2], wc[:, :, c].unsqueeze(2).to_broadcast([128, 2, 128]), MUL))
                dve.wait_ge(S["sa_mm"], c + 1)
                if c >= 2:
                    dve.wait_ge(S["y_mm"], c - 1)
                link(tt(sa[:, c % 2], ps[:, 0, 0:256].rearrange("p (a b) -> p a b", b=128),
                        p2.rearrange("p (a n) b -> p a n b", n=NCH)[:, :, c, :], ADD), "x_ready")
                dve.wait_ge(S["s_mm"], c + 1)
                if c >= 1:
                    dve.wait_ge(S["y_mm"], c)
                for cc in range(2):
                    ins = stt(state[:, (c + 1) % 2, cc, :], ps[:, 4 + cc, 0:128], wc[:, cc, c:c + 1], decayed[:, cc, :], MUL, ADD)
                    if cc:
                        count["state_ready"] = c + 1
                        link(ins, "state_ready")
                    else:
                        link(ins)
            yb = yT[:, 2:4, :]
            dve.wait_ge(S["y_copied"], NCH)
            dve.wait_ge(S["ln_sum"], 1)
            link(tt(halves(yb), halves(yb), banks(4), SUB))
            link(tt(tmp_ln, yb, yb, MUL), "ln_sq")
            dve.wait_ge(S["ln_root"], 1)
            link(v.reciprocal(tmp_ln, tmp_ln))
            for cc in range(2):
                link(stt(yb[:, cc, :], yb[:, cc, :], col("lng", cc), tmp_ln[:, cc, :], MUL, MUL))
            link(tt(yb, yb, bonus, ADD))
            link(tt(yb, yb, gg, MUL), "rwkv_out")

            def residual(t):
                n = 128 if t < TILES else NS
                b = 2 * (t % 2)
                dve.wait_ge(S["out_mm"], t + 1)
                link(tt(x[0:n, t, :], x[0:n, t, :], ps[0:n, b:b + 2, :].rearrange("p a b -> p (a b)"), ADD), "x1_done")
                mean(t, "sq2", "mean2")
                dve.wait_ge(S["root2"], t + 1)
                link(v.reciprocal(st[0:n, 3, t:t + 1], st[0:n, 2, t:t + 1]))
                link(stt(xn[0:n, t, :], x[0:n, t, :], st[0:n, 3, t:t + 1], rows[0:n, 0, :], MUL, MUL), "xn2_done")
                dve.wait_ge(S["turned2"], t + 1)
                link(v.tensor_copy(hT[:, :, 128 * t:128 * t + n],
                                   ps[:, 6:8, :].rearrange("p a (b c) -> p (a b) c", c=128)[:, :, 0:n]), "hT2_done")

            chain = [0]

            def loop_link(ins, base):
                chain[0] += 1
                v.drain()

            def choose(w, t, base, piece):
                n = 128 if t < TILES else 64

                def lk(ins):
                    loop_link(ins, base)

                if piece in (0, 1):
                    half = piece
                    if t < TILES:
                        if half == 0:
                            dve.wait_ge(S["score_mm"], w + 1)
                            lk(v.tensor_copy(scores[0:n], ps[0:n, 5, 0:256]))
                        sc = scores[0:n, 128 * half:128 * half + 128]
                    else:
                        sc = sscore[0:n, half, :]
                    a8, b8 = v16[0:n, half, 0:8], v16[0:n, half, 8:16]
                    lk(v.max(a8, sc))
                    lk(v.max_index(i16[0:n, half, 0:8], a8, sc))
                    lk(v.match_replace(scr[0:n, 0:128], a8, sc, NEG))
                    lk(v.max(b8, scr[0:n, 0:128]))
                    ins = v.max_index(i16[0:n, half, 8:16], b8, scr[0:n, 0:128])
                    lk(ins)
                    if half == 1 and t < TILES:
                        ins = ts(i16f[0:n, 0, :], i16[0:n, 0, :], 128.0, MUL)
                        ins.then_inc(S["score_used"], 1)
                        dve.wait_ge(S["score_used"], w + 1)
                    elif half == 1:
                        lk(ts(i16f[0:n, 0, :], i16[0:n, 0, :], 128.0, MUL))
                elif piece == 2:
                    lk(v.tensor_copy(i16f[0:n, 1, :], i16[0:n, 1, :]))
                    lk(tt(cand[0:n], v16[0:n, 0, :].unsqueeze(2).to_broadcast([n, TOPK, TOPK]),
                          v16[0:n, 1, :].unsqueeze(1).to_broadcast([n, TOPK, TOPK]), ADD))
                    lk(v.max(sc16[0:n, 0:8], candf[0:n]))
                    lk(v.max_index(pos[0:n, 0:8], sc16[0:n, 0:8], candf[0:n]))
                    lk(v.match_replace(scr[0:n], sc16[0:n, 0:8], candf[0:n], NEG))
                elif piece == 3:
                    lk(v.max(sc16[0:n, 8:16], scr[0:n]))
                    lk(v.max_index(pos[0:n, 8:16], sc16[0:n, 8:16], scr[0:n]))
                    ts(negm[0:n], sc16[0:n, 0:1], -1.0, MUL).then_inc(S["exp_in"], 1)
                    lk(v.tensor_single_scalar(abu[0:n, 0:16], pos[0:n], 4, ALU.logical_shift_right))
                    lk(v.tensor_single_scalar(abu[0:n, 16:32], pos[0:n], 15, ALU.bitwise_and))
                    lk(v.tensor_copy(abf[0:n], abu[0:n]))
                    oh = onehot[0:n].rearrange("p a b c -> p (a b) c")
                    lk(tt(oh, abf[0:n].unsqueeze(2).to_broadcast([n, 32, TOPK]),
                          cst("iota")[0:n].unsqueeze(1).to_broadcast([n, 32, TOPK]), ALU.is_equal))
                else:
                    lk(tt(onehot[0:n], onehot[0:n], i16f[0:n].unsqueeze(2).to_broadcast([n, 2, TOPK, TOPK]), MUL))
                    lk(v.tensor_reduce(ef[0:n], onehot[0:n], AX.X, ADD))
                    dve.wait_ge(S["exp2_done"], w + 1)
                    lk(v.reciprocal(ssum[0:n, 1:2], ssum[0:n, 0:1]))
                    lk(ts(gate[0:n, t, :], gate[0:n, t, :], ssum[0:n, 1:2], MUL))
                    tt(idx[0:n, t, :], ef[0:n, 0, :], ef[0:n, 1, :], ADD).then_inc(S["idx_ready"], 1)

            def sample_scores(h):
                dve.wait_ge(S["ss_mm"], h + 1)
                m = cst("hmask")[0:64, bass.ds(h, 1)] if not isinstance(h, int) else cst("hmask")[0:64, h:h + 1]
                flat = sscore[0:64].rearrange("p a b -> p (a b)")
                stt(flat, ps[0:64, 6, 0:256], m, flat, MUL, ADD).then_inc(S["ss_added"], 1)
                dve.wait_ge(S["ss_added"], h + 1)

            def unit(h, t, nxt, base):
                u = TILES * h + t
                n = 128 if t < TILES else 64
                row = xn[:, t, :] if t < TILES else xrep
                for s in range(TOPK):
                    dve.wait_ge(d_row[s % RING], 16 * (2 * u + s // RING + 1))
                    dve.wait_ge(S["dot_done"], TOPK * u + s + 1)
                    v.tensor_tensor_reduce(out=junk[0:n, s % 2], in0=ring[0:n, s % RING, 0:D], in1=row[0:n], scale=1.0, scalar=0.0,
                                           op0=MUL, op1=ADD, accum_out=hsel[0:n, t % 2, s:s + 1]).then_inc(S["dot_done"], 1)
                    if nxt:
                        if s == 7 and nxt[1] == 0:
                            sample_scores(nxt[0])
                        if s in (6, 8, 9, 11, 15):
                            choose(TILES * nxt[0] + nxt[1], nxt[1], base, (6, 8, 9, 11, 15).index(s))
                    if s == 3 and t:
                        add_unit(u - 1, t - 1)

            def add_unit(u, t):
                b = 2 * (t % 2)
                m = 128 if t < TILES else NS
                dve.wait_ge(S["slot_used"], TOPK * (u + 1) + RING)
                tt(x[0:m, t, :], x[0:m, t, :], ps[0:m, b:b + 2, :].rearrange("p a b -> p (a b)"), ADD)\
                    .then_inc(S["unit_added"], 1)

            dve.sem_inc(S["dot_done"], 2)
            link(v.memset(sscore[0:64], 0.0))
            dve.wait_ge(d_rows, 32)
            dve.wait_ge(d_out, 16 * 6)
            dve.wait_ge(d_swkv, 16)
            for t in range(TILES + 1):
                residual(t)
                if t < LEAD:
                    for piece in range(5):
                        choose(t, t, 0, piece)
            sample_scores(0)
            first = chain[0]
            per_choice = first // LEAD
            per_head = per_choice * TILES
            with dve.Fori(0, HEADS - 1) as h:
                chain[0] = 0
                for t in range(TILES):
                    nxt = (h, t + LEAD) if t + LEAD < TILES else (h + 1, t + LEAD - TILES)
                    unit(h, t, nxt, first + h * per_head)
                add_unit(TILES * h + TILES - 1, TILES - 1)
                assert chain[0] == per_head
            last_h = HEADS - 1
            chain[0] = 0
            for t in range(TILES):
                nxt = (last_h, t + LEAD) if t + LEAD <= TILES else None
                unit(last_h, t, nxt, first + last_h * per_head)
            unit(last_h, TILES, None, 0)
            add_unit(TILES * HEADS, TILES)
            for t in range(TILES + 1):
                n = 128 if t < TILES else NS
                mean(t, "fin_sq", "fin_mean")
                dve.wait_ge(S["fin_root"], t + 1)
                link(v.reciprocal(st[0:n, 3, t:t + 1], st[0:n, 2, t:t + 1]))
                link(stt(xn[0:n, t, :], x[0:n, t, :], st[0:n, 3, t:t + 1], rows[0:n, 1, :], MUL, MUL), "fin_done")

        @block.gpsimd
        def _(pool):
            MUL, ADD, SUB = ALU.mult, ALU.add, ALU.subtract
            count = [0]

            def link(ins):
                count[0] += 1
                ins.then_inc(pool_chain, 1)
                pool.wait_ge(pool_chain, count[0])

            def tt(out, i0, i1, op):
                return pool.tensor_tensor(out, i0, i1, op)

            pool.memset(carrier, 0.0).then_inc(S["carried"], 1)
            pool.wait_ge(d_shift, 16)
            pool.wait_ge(S["xs_done"], 7)
            pool.memset(k_bd, 0.0).then_inc(S["zero_k"], 1)
            pool.wait_ge(S["conf_out"], 1)
            pool.memset(a_bd, 0.0)
            pool.memset(b_bd, 0.0).then_inc(S["zero_ab"], 1)
            pool.wait_ge(S["exp_done"], 1)
            pool.memset(v_bd, 0.0).then_inc(S["zero_v"], 1)
            pool.wait_ge(S["z_done"], NZ)
            pool.memset(state, 0.0).then_inc(S["state_ready"], 1)

            pool.wait_ge(S["z_copied"], NZ)
            pool.wait_ge(d_small, 16 * 6)
            zd = z[:, Z_D:Z_D + 2, :]
            link(pool.memset(ppad[:, :, 0:PB], 0.0))
            link(pool.tensor_copy(ppad[:, :, PB:], zd[:, :, 0:SEQ]))
            link(pool.tensor_copy(extp[:, :, :, PB], zd[:, :, SEQ:NT]))
            pool.tensor_copy(tails[:, :, 30:45], zd[:, :, SEQ - PB:SEQ]).then_inc(S["tails_done"], 1)
            inv = cst("invcnt").rearrange("p (a b) -> p a b", b=16)
            src, esrc, lost = ppad, extp, 0
            for lv, (dst, edst) in enumerate(((pa, ea), (pb, eb), (pa, ea), (pb, eb))):
                sh = 1 << lv
                lost += sh
                link(tt(dst[:, :, lost:W], src[:, :, lost:W], src[:, :, lost - sh:W - sh], ADD))
                link(tt(edst[:, :, :, lost:], esrc[:, :, :, lost:], esrc[:, :, :, lost - sh:PB + 1 - sh], ADD))
                r, cc = slice(64 * (lv % 2), 64 * (lv % 2) + 64), lv // 2
                tt(pw[r, cc, 0:16], dst[r, cc, PB:PB + 16], inv[r, cc, :], MUL)
                tt(pw[r, cc, 16:SEQ], dst[r, cc, PB + 16:W], inv[r, cc, 15:16].to_broadcast([64, SEQ - 16]), MUL)
                link(tt(pw[r, cc, SEQ:NT], edst[r, cc, :, PB], inv[r, cc, 15:16].to_broadcast([64, NS]), MUL))
                src, esrc = dst, edst
            tt(pw, pw, zd, SUB).then_inc(S["pool_in"], 1)

            def over_values(i):
                return smp[:, i].unsqueeze(3).to_broadcast([128, 2, NS, CH])

            pool.wait_ge(d_sst, 16)
            pool.wait_ge(S["smp_ready"], 1)
            tt(sp, sst, over_values(0), MUL).then_inc(S["sample_in"], 1)
            link(tt(sst, sst, over_values(5), MUL))
            zb, zc, zh = (z[:, i:i + 2, :] for i in (Z_B, Z_C, Z_H))
            sw = col("sw", 0, 2 * SK).rearrange("p (a b) -> p a b", b=SK)
            pool.wait_ge(S["pool_in"], 1)
            link(pool.memset(qpad[:, :, 0:SK - 1], 0.0))
            link(tt(qpad[:, :, SK - 1:], zc[:, :, 0:SEQ], zh[:, :, 0:SEQ], MUL))
            link(tt(extq[:, :, :, SK - 1], zc[:, :, SEQ:NT], zh[:, :, SEQ:NT], MUL))
            pool.tensor_copy(tails[:, :, 45:47], qpad[:, :, SEQ:SEQ + 2]).then_inc(S["tails_done"], 1)
            for k in range(SK):
                o = yT[:, 4:6, :] if k == 0 else None
                wk = sw[:, :, k:k + 1]
                link(tt(yT[:, 4:6, 0:SEQ] if k == 0 else qtmp, qpad[:, :, k:k + SEQ], wk.to_broadcast([128, 2, SEQ]), MUL))
                link(tt(yT[:, 4:6, SEQ:NT] if k == 0 else qs, extq[:, :, :, k], wk.to_broadcast([128, 2, NS]), MUL))
                if k:
                    link(tt(yT[:, 4:6, 0:SEQ], yT[:, 4:6, 0:SEQ], qtmp, ADD))
                    link(tt(yT[:, 4:6, SEQ:NT], yT[:, 4:6, SEQ:NT], qs, ADD))
            tt(yT[:, 4:6, :], yT[:, 4:6, :], zb, MUL).then_inc(S["short_done"], 1)
            pool.wait_ge(S["sample_copied"], 1)
            link(tt(sp, ssp, over_values(1), MUL))
            link(tt(sst, sst, sp, ADD))
            for cc in range(2):
                last = tt(sp[:, cc], imask.unsqueeze(1).to_broadcast([128, NS, CH]),
                          smp[:, 4, cc, :].unsqueeze(2).to_broadcast([128, NS, CH]), MUL)
            last.then_inc(S["sample_in"], 1)
            pool.wait_ge(S["sample_copied"], 2)
            link(tt(sp, ssp, over_values(2), MUL))
            link(tt(sst, sst, sp, ADD))
            tt(sp, sst, over_values(3), MUL).then_inc(S["sample_in"], 1)
            pool.wait_ge(S["sample_in"], 3)
            pool.tensor_copy(carrier[:, 1:2], carrier[:, 0:1]).then_inc(S["samp_state"], 1)

            def gathers(h, t):
                u = TILES * h + t
                n = 128 if t < TILES else 64
                pool.wait_ge(S["idx_ready"], u + 1)
                for s in range(TOPK):
                    if s % 2 == 0:
                        pool.wait_ge(S["slot_used"], TOPK * u + s + 2)
                        pool.wait_ge(S["carried"], TOPK // 2 * u + s // 2 + 1)
                        pool.tensor_tensor(carrier[:, 1:2], carrier[:, 0:1], carrier[:, 0:1], ALU.add).then_inc(S["carried"], 1)
                    pool.indirect_dma_start(
                        out=ring[0:n, s % RING, :], out_offset=None, in_=a["uv"][:, :],
                        in_offset=bass.IndirectOffsetOnAxis(ap=idx[0:n, t, s:s + 1], axis=0),
                    ).then_inc(d_row[s % RING], 16)

            with pool.Fori(0, HEADS) as h:
                for t in range(TILES):
                    gathers(h, t)
            gathers(HEADS - 1, TILES)


def kernel(**inputs):
    import concourse.bacc as bacc
    from concourse.bass_utils import run_bass_kernel_spmd as run

    i = {k: np.asarray(v) for k, v in inputs.items()}
    order = column_order()

    def chans(v, lead=()):
        return np.asarray(v).reshape(-1, 128).T

    def per_chunk(v):
        v = np.moveaxis(v, -1, 0)
        return np.ascontiguousarray(v.reshape((-1, 128) + v.shape[1:]).swapaxes(0, 1))

    rw = order[512:512 + 896] - 512
    packed = {
        "g1": chans(i["norm1_g"][0]), "mu": chans(i["rwkv_mu"][0][rw]), "w0": chans(i["rwkv_w0"][0]),
        "a0": chans(i["rwkv_a0"][0]), "kk": chans(i["rwkv_k_k"][0]), "ka": chans(i["rwkv_k_a"][0]),
        "rk": chans(i["rwkv_r_k"][0].reshape(-1)), "lng": chans(i["rwkv_ln_g"][0]), "lnb": chans(i["rwkv_ln_b"][0]),
        "cw": per_chunk(i["conf_dw_w"][0]).reshape(128, -1), "cb": chans(i["conf_dw_b"][0]),
        "clg": chans(i["conf_ln_g"][0]), "clb": chans(i["conf_ln_b"][0]),
        "sw": per_chunk(i["sc_conv_w"][0]).reshape(128, -1), "ps": chans(i["pool_scale"][0]),
    }
    poolw = np.zeros((128, 2, 128), np.float32)
    for g in range(4):
        p = 64 * (g % 2)
        poolw[p:p + 64, g // 2, p:p + 64] = i["pool_w"][0, g]
    wqk = np.concatenate([
        i["peer_wq"][0].reshape(8, 128, HEADS, 256).transpose(2, 1, 0, 3).reshape(HEADS, 128, -1),
        i["peer_k1"][0].transpose(0, 2, 1), i["peer_k2"][0].transpose(0, 2, 1)], -1)
    wkv = i["state_rwkv_wkv"][0].reshape(NS, 2, 2, 64, 64)
    arrays = {
        "const": constants(),
        "cols": np.concatenate([packed[n] for n in COLUMNS], 1),
        "xp": i["x_prompt"][0], "xs": i["x_sample"][:, 0],
        "win": i["w_in"][0][:, order].reshape(KT, 128, NZ, 128).transpose(2, 1, 0, 3).reshape(NZ, 128, -1),
        "wout": i["w_out"][0].reshape(KT, 128, D).transpose(1, 0, 2),
        "wqk": wqk,
        "uv": np.concatenate([i["peer_u"][0], i["peer_v"][0]], 1),
        "n2": i["norm2_g"], "nf": i["final_norm_g"][None],
        "sconf": per_chunk(i["state_conformer"][0]), "spool": per_chunk(i["state_pool"][0]),
        "ssc": per_chunk(i["state_shortconv"][0]), "sshift": per_chunk(i["state_rwkv_shift"][0][:, rw]),
        "lora": np.concatenate([i["rwkv_w2"][0], i["rwkv_a2"][0], i["rwkv_g2"][0]], 0),
        "poolw": poolw,
        "swkv": wkv.transpose(2, 4, 1, 0, 3).reshape(128, 2, NS, 64),
    }
    outs = {
        "yp": (SEQ, D), "ys": (NS, D), "o_shift": (128, 7, 9), "o_tails": (128, 2 * 47),
        "o_sconf": (128, 2, NS, 30), "o_spool": (128, 2, NS, 15), "o_ssc": (128, 2, NS, 2),
        "o_swkv": (128, 2, NS, 64), "o_wkv": (128, 2, 64),
    }
    nc = bacc.Bacc("TRN2", target_bir_lowering=False, num_devices=1)
    feed, args = {}, {}
    for name, arr in arrays.items():
        arr = np.ascontiguousarray(arr)
        feed["in_" + name] = arr
        args[name] = nc.dram_tensor("in_" + name, arr.shape, mybir.dt.from_np(arr.dtype), kind="ExternalInput").ap()
    for name, shape in outs.items():
        args[name] = nc.dram_tensor("out_" + name, shape, F32, kind="ExternalOutput").ap()
    build(nc, args)
    r = run(nc, [feed], core_ids=[0]).results[0]
    o = {name: np.asarray(r["out_" + name]) for name in outs}

    def rows_of(v):
        v = v.swapaxes(0, 1)
        return np.ascontiguousarray(np.moveaxis(v.reshape((-1,) + v.shape[2:]), 0, -1))

    shift = rows_of(o["o_shift"])
    back = np.empty_like(shift)
    back[:, rw] = shift
    tails = o["o_tails"].reshape(128, 2, 47)
    wkv_p = o["o_wkv"].reshape(2, 64, 2, 64).transpose(2, 0, 3, 1).reshape(4, 64, 64)
    wkv_s = o["o_swkv"].reshape(2, 64, 2, NS, 64).transpose(3, 2, 0, 4, 1).reshape(NS, 4, 64, 64)
    return (
        o["yp"][None], o["ys"][:, None],
        rows_of(tails[:, :, 0:30])[None, None], rows_of(o["o_sconf"])[None],
        back[0][None, None], back[1:][None],
        wkv_p[None, None], wkv_s[None],
        rows_of(tails[:, :, 45:47])[None, None], rows_of(o["o_ssc"])[None],
        rows_of(tails[:, :, 30:45])[None, None], rows_of(o["o_spool"])[None],
    )
```
